# Optimizing a Trainium2 kernel written in Bass

```python
import jax, jax.numpy as jnp
from jax import lax
import numpy as np

D_MODEL = 2048
BATCH = 1
SEQ = 256
DEPTH = 1
DEC_BATCH = 8
DEC_SEQ = 8
PAST_LEN = 2048
PAGE_SIZE = 128

N_MEM = 256
CONV_DIM = 1024
CONV_K = 31
DN_HEADS = 16
DN_HEAD_DIM = 128
DN_DIM = DN_HEADS * DN_HEAD_DIM
DN_CONV_K = 4
DN_CHUNK = 64
XA_HEADS = 4
XA_HEAD_DIM = 256
XA_DIM = XA_HEADS * XA_HEAD_DIM
PEER_HEADS = 8
PEER_N_KEYS = 128
PEER_N_EXPERTS = PEER_N_KEYS * PEER_N_KEYS
PEER_DK = 256
PEER_TOPK = 16
PEER_BLOCK = 128
NORM_EPS = 1e-6

IN_SIZES = (CONV_DIM, CONV_DIM, 3 * DN_DIM, DN_DIM, DN_HEADS, DN_HEADS, XA_DIM, D_MODEL, D_MODEL, D_MODEL)
IN_COLS = sum(IN_SIZES)
IN_SPLITS = tuple(sum(IN_SIZES[:i + 1]) for i in range(len(IN_SIZES) - 1))

kernel_name = 'hybrid_conformer_gdn_peer_decode_step'

def rms_norm(x, g):
    xf = x.astype(jnp.float32)
    xf = xf * lax.rsqrt(jnp.mean(xf * xf, axis=-1, keepdims=True) + NORM_EPS)
    return xf.astype(x.dtype) * g

def layer_norm(x, g, b):
    xf = x.astype(jnp.float32)
    mu = jnp.mean(xf, axis=-1, keepdims=True)
    xc = xf - mu
    var = jnp.mean(xc * xc, axis=-1, keepdims=True)
    return (xc * lax.rsqrt(var + NORM_EPS)).astype(x.dtype) * g + b

def l2_normalize(x):
    xf = x.astype(jnp.float32)
    return xf * lax.rsqrt(jnp.sum(xf * xf, axis=-1, keepdims=True) + NORM_EPS)

def causal_depthwise_conv(buf, x, w):
    k = w.shape[0]
    xp = jnp.concatenate([buf.astype(x.dtype), x], axis=1)
    y = lax.conv_general_dilated(xp, w[:, None, :].astype(x.dtype), window_strides=(1,), padding='VALID',
                                 dimension_numbers=('NWC', 'WIO', 'NWC'), feature_group_count=x.shape[-1])
    return y, xp[:, xp.shape[1] - (k - 1):]

def gated_delta_chunked(q, k, v, g, beta, state):
    b, l, h, _ = q.shape
    dv = v.shape[-1]
    c = min(DN_CHUNK, l)
    pad = (-l) % c
    n = (l + pad) // c

    def blocks(t):
        t = jnp.pad(t, [(0, 0), (0, pad)] + [(0, 0)] * (t.ndim - 2))
        t = t.reshape((b, n, c) + t.shape[2:])
        return jnp.moveaxis(t, 3, 1)

    q, k, v, g, beta = blocks(q), blocks(k), blocks(v), blocks(g), blocks(beta)
    gc = jnp.cumsum(g, axis=-1)
    idx = jnp.arange(c)
    incl = idx[:, None] >= idx[None, :]
    strict = idx[:, None] > idx[None, :]
    decay_incl = jnp.exp(jnp.where(incl, gc[..., :, None] - gc[..., None, :], -jnp.inf))
    decay_strict = jnp.where(strict, decay_incl, 0.0)
    kb = k * beta[..., None]
    a_mat = jnp.einsum('bhncd,bhnjd->bhncj', kb, k) * decay_strict
    rhs = jnp.concatenate([v * beta[..., None], kb * jnp.exp(gc)[..., None]], axis=-1)
    sol = lax.linalg.triangular_solve(a_mat + jnp.eye(c, dtype=a_mat.dtype), rhs, left_side=True,
                                      lower=True, unit_diagonal=True)
    value, k_cum = sol[..., :dv], sol[..., dv:]
    qk = jnp.einsum('bhncd,bhnjd->bhncj', q, k) * decay_incl
    q_dec = q * jnp.exp(gc)[..., None]
    k_dec = k * jnp.exp(gc[..., -1:] - gc)[..., None]
    g_last = jnp.exp(gc[..., -1])
    xs = tuple(jnp.moveaxis(t, 2, 0) for t in (value, k_cum, qk, q_dec, k_dec, g_last))

    def step(s, inp):
        val, kc, qk_c, qd, kd, gl = inp
        u = val - jnp.einsum('bhcd,bhde->bhce', kc, s)
        o = jnp.einsum('bhcd,bhde->bhce', qd, s) + jnp.einsum('bhcj,bhje->bhce', qk_c, u)
        s = s * gl[..., None, None] + jnp.einsum('bhcd,bhce->bhde', kd, u)
        return s, o

    state, o = lax.scan(step, state, xs)
    o = jnp.transpose(o, (1, 0, 3, 2, 4)).reshape(b, n * c, h, dv)[:, :l]
    return o, state

def memory_kv(mem, norm_mem, w_mem_kv):
    b, m, _ = mem.shape
    kv = rms_norm(mem, norm_mem) @ w_mem_kv
    k, v = jnp.split(kv, 2, axis=-1)
    return k.reshape(b, m, XA_HEADS, XA_HEAD_DIM), v.reshape(b, m, XA_HEADS, XA_HEAD_DIM)

def memory_attention(q, mem_k, mem_v):
    b, l, _ = q.shape
    q = q.reshape(b, l, XA_HEADS, XA_HEAD_DIM)
    s = jnp.einsum('blhd,bmhd->bhlm', q, mem_k.astype(q.dtype)).astype(jnp.float32) * (XA_HEAD_DIM ** -0.5)
    p = jax.nn.softmax(s, axis=-1).astype(q.dtype)
    o = jnp.einsum('bhlm,bmhd->blhd', p, mem_v.astype(q.dtype))
    return o.reshape(b, l, XA_DIM)

def peer_ffn(h, w_q, keys_1, keys_2, expert_u, expert_v):
    shp = h.shape
    xt = h.reshape(-1, D_MODEL)
    n = xt.shape[0]
    pad = (-n) % PEER_BLOCK
    xb = jnp.pad(xt, ((0, pad), (0, 0))).reshape(-1, PEER_BLOCK, D_MODEL)
    k1 = keys_1.astype(jnp.float32)
    k2 = keys_2.astype(jnp.float32)

    def block(xblk):
        q = (xblk @ w_q).astype(jnp.float32).reshape(PEER_BLOCK, PEER_HEADS, 2, PEER_DK // 2)
        s1 = jnp.einsum('thd,kd->thk', q[:, :, 0], k1)
        s2 = jnp.einsum('thd,kd->thk', q[:, :, 1], k2)
        t1, i1 = lax.top_k(s1, PEER_TOPK)
        t2, i2 = lax.top_k(s2, PEER_TOPK)
        cand = (t1[..., :, None] + t2[..., None, :]).reshape(PEER_BLOCK, PEER_HEADS, PEER_TOPK * PEER_TOPK)
        cidx = (i1[..., :, None] * PEER_N_KEYS + i2[..., None, :]).reshape(PEER_BLOCK, PEER_HEADS, PEER_TOPK * PEER_TOPK)
        top, pos = lax.top_k(cand, PEER_TOPK)
        eidx = jnp.take_along_axis(cidx, pos, axis=-1)
        gate = jax.nn.softmax(top, axis=-1).astype(xblk.dtype)
        u = expert_u[eidx]
        act = jax.nn.gelu(jnp.einsum('td,thkd->thk', xblk, u))
        v = expert_v[eidx]
        return jnp.einsum('thk,thkd->td', gate * act, v)

    out = lax.map(block, xb)
    return out.reshape(-1, D_MODEL)[:n].reshape(shp)

def hybrid_layer(x, mem_k, mem_v, conv_buf, qkv_buf, delta_state,
                 norm_mix, w_in, conv_dw, conv_dw_b, conv_ln_g, conv_ln_b, w_conv_out,
                 dn_conv_w, dn_a_log, dn_dt_bias, dn_norm_g, w_dn_out, w_xa_out, w_out,
                 norm_ffn, w_peer_q, peer_keys_1, peer_keys_2, peer_u, peer_v):
    b, l, _ = x.shape
    h = rms_norm(x, norm_mix)
    proj = h @ w_in
    (glu_a, glu_g, qkv, z, a_raw, b_raw, xq,
     gate_conv, gate_dn, gate_xa) = jnp.split(proj, IN_SPLITS, axis=-1)
    u = glu_a * jax.nn.sigmoid(glu_g)
    c, new_conv_buf = causal_depthwise_conv(conv_buf, u, conv_dw)
    c = jax.nn.silu(layer_norm(c + conv_dw_b, conv_ln_g, conv_ln_b))
    y_conv = c @ w_conv_out
    qkv_c, new_qkv_buf = causal_depthwise_conv(qkv_buf, qkv, dn_conv_w)
    qkv_c = jax.nn.silu(qkv_c)
    q, k, v = (t.reshape(b, l, DN_HEADS, DN_HEAD_DIM) for t in jnp.split(qkv_c, 3, axis=-1))
    q = l2_normalize(q) * (DN_HEAD_DIM ** -0.5)
    k = l2_normalize(k)
    g = -jnp.exp(dn_a_log.astype(jnp.float32)) * jax.nn.softplus(a_raw.astype(jnp.float32) + dn_dt_bias.astype(jnp.float32))
    beta = jax.nn.sigmoid(b_raw.astype(jnp.float32))
    o, new_state = gated_delta_chunked(q, k, v.astype(jnp.float32), g, beta, delta_state.astype(jnp.float32))
    o = rms_norm(o.astype(x.dtype), dn_norm_g) * jax.nn.silu(z.reshape(b, l, DN_HEADS, DN_HEAD_DIM))
    y_dn = o.reshape(b, l, DN_DIM) @ w_dn_out
    y_xa = memory_attention(xq, mem_k, mem_v) @ w_xa_out
    merged = (jax.nn.sigmoid(gate_conv) * y_conv + jax.nn.sigmoid(gate_dn) * y_dn
              + jax.nn.sigmoid(gate_xa) * y_xa)
    x = x + merged @ w_out
    x = x + peer_ffn(rms_norm(x, norm_ffn), w_peer_q, peer_keys_1, peer_keys_2, peer_u, peer_v)
    return x, new_conv_buf, new_qkv_buf, new_state.astype(delta_state.dtype)

def setup_inputs(seed: int = 0) -> dict:
    key = jax.random.key(seed)
    ks = iter(jax.random.split(key, 48))
    f32 = jnp.float32
    L = DEPTH

    def nrm(shape, scale):
        return jax.random.normal(next(ks), shape, f32) * scale

    def gain(shape):
        return 1.0 + nrm(shape, 0.02)

    return {
        'x_prompt': nrm((BATCH, SEQ, D_MODEL), 1.0),
        'x_sample': nrm((DEC_BATCH, DEC_SEQ, D_MODEL), 1.0),
        'mem_prompt': nrm((BATCH, N_MEM, D_MODEL), 1.0),
        'cache_mem_k': nrm((L, DEC_BATCH, N_MEM, XA_HEADS, XA_HEAD_DIM), 1.0),
        'cache_mem_v': nrm((L, DEC_BATCH, N_MEM, XA_HEADS, XA_HEAD_DIM), 1.0),
        'state_conv': nrm((L, DEC_BATCH, CONV_K - 1, CONV_DIM), 1.0),
        'state_qkv_conv': nrm((L, DEC_BATCH, DN_CONV_K - 1, 3 * DN_DIM), 1.0),
        'state_delta': nrm((L, DEC_BATCH, DN_HEADS, DN_HEAD_DIM, DN_HEAD_DIM), 0.1),
        'norm_mix': gain((L, D_MODEL)),
        'norm_mem': gain((L, D_MODEL)),
        'w_in': nrm((L, D_MODEL, IN_COLS), D_MODEL ** -0.5),
        'conv_dw': nrm((L, CONV_K, CONV_DIM), CONV_K ** -0.5),
        'conv_dw_b': nrm((L, CONV_DIM), 0.02),
        'conv_ln_g': gain((L, CONV_DIM)),
        'conv_ln_b': nrm((L, CONV_DIM), 0.02),
        'w_conv_out': nrm((L, CONV_DIM, D_MODEL), CONV_DIM ** -0.5),
        'dn_conv_w': nrm((L, DN_CONV_K, 3 * DN_DIM), DN_CONV_K ** -0.5),
        'dn_a_log': jnp.log(jax.random.uniform(next(ks), (L, DN_HEADS), f32, 1.0, 16.0)),
        'dn_dt_bias': jnp.log(jnp.expm1(jax.random.uniform(next(ks), (L, DN_HEADS), f32, 0.001, 0.1))),
        'dn_norm_g': gain((L, DN_HEAD_DIM)),
        'w_dn_out': nrm((L, DN_DIM, D_MODEL), DN_DIM ** -0.5),
        'w_mem_kv': nrm((L, D_MODEL, 2 * XA_DIM), D_MODEL ** -0.5),
        'w_xa_out': nrm((L, XA_DIM, D_MODEL), XA_DIM ** -0.5),
        'w_out': nrm((L, D_MODEL, D_MODEL), D_MODEL ** -0.5),
        'norm_ffn': gain((L, D_MODEL)),
        'w_peer_q': nrm((L, D_MODEL, PEER_HEADS * PEER_DK), D_MODEL ** -0.5),
        'peer_keys_1': nrm((L, PEER_N_KEYS, PEER_DK // 2), (PEER_DK // 2) ** -0.5),
        'peer_keys_2': nrm((L, PEER_N_KEYS, PEER_DK // 2), (PEER_DK // 2) ** -0.5),
        'peer_u': nrm((L, PEER_N_EXPERTS, D_MODEL), D_MODEL ** -0.5),
        'peer_v': nrm((L, PEER_N_EXPERTS, D_MODEL), PEER_HEADS ** -0.5),
        'norm_final': gain((D_MODEL,)),
    }

def reference(x_prompt, x_sample, mem_prompt, cache_mem_k, cache_mem_v, state_conv, state_qkv_conv, state_delta,
              norm_mix, norm_mem, w_in, conv_dw, conv_dw_b, conv_ln_g, conv_ln_b, w_conv_out,
              dn_conv_w, dn_a_log, dn_dt_bias, dn_norm_g, w_dn_out, w_mem_kv, w_xa_out, w_out,
              norm_ffn, w_peer_q, peer_keys_1, peer_keys_2, peer_u, peer_v, norm_final):
    bp = x_prompt.shape[0]
    dt = x_prompt.dtype
    xp, xs = x_prompt, x_sample
    mk_p, mv_p, conv_p, qkv_p, delta_p, conv_s, qkv_s, delta_s = [], [], [], [], [], [], [], []
    for i in range(DEPTH):
        lw = (norm_mix[i], w_in[i], conv_dw[i], conv_dw_b[i], conv_ln_g[i], conv_ln_b[i], w_conv_out[i],
              dn_conv_w[i], dn_a_log[i], dn_dt_bias[i], dn_norm_g[i], w_dn_out[i], w_xa_out[i], w_out[i],
              norm_ffn[i], w_peer_q[i], peer_keys_1[i], peer_keys_2[i], peer_u[i], peer_v[i])
        mk, mv = memory_kv(mem_prompt, norm_mem[i], w_mem_kv[i])
        xp, cb, qb, st = hybrid_layer(
            xp, mk, mv,
            jnp.zeros((bp, CONV_K - 1, CONV_DIM), dt),
            jnp.zeros((bp, DN_CONV_K - 1, 3 * DN_DIM), dt),
            jnp.zeros((bp, DN_HEADS, DN_HEAD_DIM, DN_HEAD_DIM), jnp.float32),
            *lw)
        mk_p.append(mk)
        mv_p.append(mv)
        conv_p.append(cb)
        qkv_p.append(qb)
        delta_p.append(st)
        xs, cb2, qb2, st2 = hybrid_layer(
            xs, cache_mem_k[i], cache_mem_v[i], state_conv[i], state_qkv_conv[i], state_delta[i], *lw)
        conv_s.append(cb2)
        qkv_s.append(qb2)
        delta_s.append(st2)
    y_prompt = rms_norm(xp, norm_final)
    y_sample = rms_norm(xs, norm_final)
    return (y_prompt, y_sample, jnp.stack(mk_p), jnp.stack(mv_p), jnp.stack(conv_p), jnp.stack(qkv_p),
            jnp.stack(delta_p), jnp.stack(conv_s), jnp.stack(qkv_s), jnp.stack(delta_s))


_drawn_inputs = setup_inputs


def setup_inputs(seed=0):
    import zlib

    import numpy as np

    out = dict(_drawn_inputs(seed))
    spreads = {}
    factors = {'norm_mem': 7.733,
     'conv_ln_g': 34.019,
     'conv_ln_b': 35.165,
     'dn_norm_g': 47.274,
     'norm_final': 21.254,
     'norm_ffn': 15.133,
     'cache_mem_k': 5.995,
     'cache_mem_v': 4.842}
    for name, (base, spread) in spreads.items():
        noise = np.random.default_rng([zlib.crc32(name.encode()), seed]).standard_normal(out[name].shape)
        drawn = base * np.exp(spread * noise) if base else spread * noise
        out[name] = __import__('jax').numpy.asarray(drawn.astype(out[name].dtype))
    for name, factor in factors.items():
        out[name] = (out[name] * factor).astype(out[name].dtype)
    return out
```

```python
from contextlib import ExitStack

import numpy as np
import concourse.bass as bass
from concourse import mybir

F32 = mybir.dt.float32
BF16 = mybir.dt.bfloat16
U32 = mybir.dt.uint32
I32 = mybir.dt.int32
ACT = mybir.ActivationFunctionType
ALU = mybir.AluOpType
AX = mybir.AxisListType.X

P = 128
D = 2048
KT = D // P
TP, NBATCH, TS = 256, 8, 8
NS = NBATCH * TS
TOKENS = TP + NS
MEM = 256
CT = 1024 // P
CK = 31
CWIN_S = CK - 1 + TS
CWIN = CK - 1 + TP + NBATCH * CWIN_S
H = 16
QK = 4
QWIN_S = QK - 1 + TS
QWIN0 = QK - 1 + TP
QWIN = QWIN0 + NBATCH * QWIN_S
AH = 4
PH = 8
NK = 128
TOPK = 16
EPS = 1e-6
NEG = -3.0e38
UNITS = 3
UT = UNITS * P

GC, BETA, NBEG, KDEC, EGL, EGLB, GRAW, NHP = 0, 3, 6, 9, 12, 14, 22, 25
C_MEM, C_MIX, C_FFN, C_LNG, C_LNB, C_DWB, C_DW = 0, 16, 32, 48, 56, 64, 72
C_DNW = C_DW + CT * CK
C_DNG = C_DNW + H * 3 * QK
C_ALL = C_DNG + 1

STREAM = [("kv", 4, 4), ("glu", 4, 4), ("head", H, 4), ("att", AH, 6), ("merge", KT, 5), ("out", 4, 4), ("pq", 4, 4)]
AHEAD = 4


def stream_plan():
    first, before, n, per_slot = {}, {}, 0, [0] * 8
    for name, iters, tiles in STREAM:
        first[name], before[name] = n, list(per_slot)
        n += iters * tiles
        for s in range(tiles):
            per_slot[s] += iters
    return first, before


FIRST, BEFORE = stream_plan()
LEVELS = [1, 2, 4, 8, 16, 32, 64]
T_STEPS = 2 * len(LEVELS) - 1
HEAD_STEPS = 30
TOPK_STEPS = 116
SAMPLE_LEVELS = 3


class Steps:

    def __init__(self, eng, sem):
        self.eng, self.sem, self.base, self.n, self.total = eng, sem, 0, 0, 0

    def __call__(self, ins):
        self.n += 1
        ins.then_inc(self.sem, 1)
        return self.n

    def wait(self, n=None):
        self.eng.wait_ge(self.sem, self.base + (self.n if n is None else n))

    def wait_after(self, sem, count):
        self.eng.to_reg(self.base + self.n)
        self.eng.wait_ge(sem, count)
        self.wait()

    def enter(self, i, per):
        self.start, self.per = self.n + self.base, per
        self.base, self.n = self.start + i * per, 0

    def leave(self, iters):
        assert self.n == self.per, ("steps per iteration", self.n)
        self.base, self.n = 0, self.start + iters * self.per


def build(nc, io):
    with ExitStack() as ctx:
        def sb(name, shape, dt=F32):
            return ctx.enter_context(nc.sbuf_tensor(name, shape, dt))

        def sem(name):
            return ctx.enter_context(nc.semaphore(name))

        def view(flat, at, *shape):
            n = int(np.prod(shape))
            v = flat[:, at[0]:at[0] + n]
            at[0] += n
            assert at[0] <= flat.shape[1], (at, flat.shape)
            return v if len(shape) == 1 else v.rearrange("p (a b) -> p a b", a=shape[0])

        ring = sb("ring", [P, 8, D])
        xT = sb("xT", [P, KT, TOKENS])
        hT = sb("hT", [P, KT, TOKENS])
        mm = sb("mm", [P, KT, TOKENS])
        kmem = sb("kmem", [P, CT, MEM])
        vmem = sb("vmem", [P, 2, 1024])
        branches = sb("branches", [P, (H + CT + CT) * TOKENS])
        oT = branches[:, 0:H * TOKENS].rearrange("p (h t) -> p h t", h=H)
        cT = branches[:, H * TOKENS:(H + CT) * TOKENS].rearrange("p (h t) -> p h t", h=CT)
        xoT = branches[:, (H + CT) * TOKENS:].rearrange("p (h t) -> p h t", h=CT)
        cst = sb("cst", [P, C_ALL])
        ones = sb("ones", [P, P])
        ident = sb("ident", [P, P])
        rs = sb("rs", [P, TOKENS])
        mean = sb("mean", [P, TOKENS])
        lm = sb("lm", [P, len(LEVELS), P])
        mu3 = sb("mu3", [P, UNITS, P])
        blk = sb("blk", [P, P])
        bm = sb("bm", [P, NBATCH])
        ab = sb("ab", [P, UNITS, 32])
        hp = sb("hp", [P, H, NHP])
        hs = sb("hs", [P, NHP])
        hs_pool = sb("hs_pool", [P, NHP])
        pw = sb("pw", [P, 3 * QK])
        egb = sb("egb", [P, UT])

        at = [0]
        vT = view(branches, at, CT, MEM)
        cwin = view(branches, at, 2, CWIN)
        sg = view(branches, at, 2, TOKENS)
        assert at[0] <= H * TOKENS
        low = ring[:, 4:6, :].rearrange("p a b -> p (a b)")
        at = [0]
        qwin, qn, kn, vv = view(low, at, 3, QWIN), view(low, at, UT), view(low, at, UT), view(low, at, UT)
        dt3, db3, gb, bb = (view(low, at, UNITS, P) for _ in range(4))
        at = [0]
        six = ring[:, 6, :]
        sin, um = view(six, at, NBATCH, P), view(six, at, NBATCH, P)
        at = [0]
        seven = ring[:, 7, :]
        knm, qkd, tt, tn = view(seven, at, NBATCH * 72), view(seven, at, UNITS, P), view(seven, at, UNITS, P), view(seven, at, UNITS, P)
        zs = view(seven, at, TOKENS)
        mmf = mm[:, :, :].rearrange("p a b -> p (a b)")
        at = [0]
        lt = view(mmf, at, len(LEVELS), UT)
        kd, vb, uu, at3, pm = (view(mmf, at, UNITS, P) for _ in range(5))
        s1, s2 = view(mmf, at, P), view(mmf, at, P)
        xof = branches[:, (H + CT) * TOKENS:]
        at = [0]
        cv, th, nrm = view(xof, at, 3, TOKENS), view(xof, at, 3, TOKENS), view(xof, at, 2, TOKENS)
        sqo = nrm[:, 0]

        psum = ctx.enter_context(nc.psum_tensor("psum", [P, 8, 512], F32))
        ps = [psum[:, i, :] for i in range(8)]

        def three(bank):
            return ps[bank][:, 0:UT].rearrange("p (a b) -> p a b", a=UNITS)

        in_mem, in_x, in_cst, in_rows, in_ab = sem("in_mem"), sem("in_x"), sem("in_cst"), sem("in_rows"), sem("in_ab")
        w_in = [sem(f"w_in{i}") for i in range(6)]
        tiles_done = sem("tiles_done")
        consts_ready = sem("consts_ready")
        pool_step, dve_step = sem("pool_step"), sem("dve_step")
        sq_ready, ss_done, ms_ready, rt_ready, norm_ready = (sem(n) for n in ("sq_ready", "ss_done", "ms_ready", "rt_ready", "norm_ready"))
        v_turned, v_placed, stored = sem("v_turned"), sem("v_placed"), sem("stored")
        ab_done, ab_ready, sp_a, sp_b, sp_c = (sem(n) for n in ("ab_done", "ab_ready", "sp_a", "sp_b", "sp_c"))

        ab_w = sb("ab_w", [P, KT * 32])
        rows = sb("rows", [P, 32])
        two = range(2)
        kv_free = [sem(f"kv_free{j}") for j in range(4)]
        conv_read, cwin_in, cwin_out = ([sem(f"{n}{j}") for j in two] for n in ("conv_read", "cwin_in", "cwin_out"))
        proj_read = [sem(f"proj_read{j}") for j in range(4)]
        o_done = sem("o_done")
        qst_in, qwin_out, sin_in, sin_out, s2_out, sn_ready, sc_done, qd_ready, silu_ready = (sem(n) for n in (
            "qst_in", "qwin_out", "sin_in", "sin_out", "s2_out", "sn_ready", "sc_done", "qd_ready", "silu_ready"))
        gate_ready, cwin_full = ([sem(f"{n}{j}") for j in two] for n in ("gate_ready", "cwin_full"))
        gz = sb("gz", [P, 48 + P])
        dwp2 = sb("dwp2", [P, 2, CK + 1])
        half = sb("half", [P, CT + 1])
        sp3 = sb("sp3", [P, 4, 48])
        ex = sb("ex", [P, 144 + P])
        sp_v, sp_s = sem("sp_v"), sem("sp_s")
        gb_ready, rows_done, rows_used, sq_qk, ssq_done, nrm_ready, nrt_ready, qk_ready = (sem(n) for n in (
            "gb_ready", "rows_done", "rows_used", "sq_qk", "ssq_done", "nrm_ready", "nrt_ready", "qk_ready"))
        g_done, tok_done, tok_read, at_ready, lt_ready, t_ready, turn_done, p_done, p_ready, dd_done = (sem(n) for n in (
            "g_done", "tok_done", "tok_read", "at_ready", "lt_ready", "t_ready", "turn_done", "p_done", "p_ready", "dd_done"))
        v_ready, tanh_ready, dtx_ready, knm_ready, ks_done, r_ready = (sem(n) for n in (
            "v_ready", "tanh_ready", "dtx_ready", "knm_ready", "ks_done", "r_ready"))
        u_done, u_ready, s_done, s1_ready, um_ready, sn_done, so_done, osq_ready, oss_done, orm_ready, ort_ready = (sem(n) for n in (
            "u_done", "u_ready", "s_done", "s1_ready", "um_ready", "sn_done", "so_done", "osq_ready", "oss_done", "orm_ready", "ort_ready"))
        dt_ready, z_ready, conv_ready, state_ready = sem("dt_ready"), sem("z_ready"), sem("conv_ready"), sem("state_ready")

        at = [0]
        xq, pp, pT = view(six, at, 2, TOKENS), view(six, at, UNITS, MEM), view(six, at, 2, TOKENS)
        qm = seven[:, 0:2 * 576].rearrange("p (t n) -> p t n", t=2)
        mx, sm, r3 = sb("mx", [P, UNITS]), sb("sm", [P, UNITS]), sb("r3", [P, UNITS])
        g3 = seven[:, 0:3 * TOKENS].rearrange("p (n t) -> p n t", n=3)
        t3 = six[:, 0:3 * TOKENS].rearrange("p (n t) -> p n t", n=3)
        lnsq = mmf[:, 0:CT * TOKENS].rearrange("p (c t) -> p c t", c=CT)
        x2tok = branches[:, 0:UNITS * D].rearrange("p (t d) -> p t d", t=UNITS)
        grow = kmem[:, :, :].rearrange("p a b -> p (a b)")
        h2 = vmem[:, :, :].rearrange("p a b -> p (a b)")
        parts = mmf.bitcast(BF16)[:, 0:3 * D].rearrange("p (n d) -> p n d", n=3)
        keys = sb("keys", [P, 2, NK])
        qs = six[:, 0:2 * TOKENS].rearrange("p (n t) -> p n t", n=2)
        at = [0]
        sc, sc2 = view(low, at, 4, UT), view(low, at, 2, UT)
        cand = view(low, at, UNITS, TOPK * TOPK)
        at = [0]
        cand2, eq = view(seven, at, UNITS, TOPK * TOPK), view(seven, at, UNITS * TOPK, TOPK)
        xflat = xT[:, :, :].rearrange("p a b -> p (a b)")
        at = [0]

        def small(*shape, dt=F32):
            v = view(xflat, at, int(np.prod(shape)))
            if dt != F32:
                v = v.bitcast(dt)
            names = "abc"[:len(shape)]
            sizes = dict(zip(names, shape))
            return v if len(shape) == 1 else v.rearrange(f"p ({' '.join(names)}) -> p {' '.join(names)}", **sizes)

        def lists(dt=F32):
            v = small(2 * UNITS * TOPK, dt=dt)
            return v.rearrange("p (x t k) -> p x t k", x=2, t=UNITS)

        v16, i16, iu = lists(), lists(), lists(U32)
        pos, digits = small(UNITS, TOPK, dt=U32), small(2, UNITS * TOPK, dt=U32)
        fdig, e12 = small(2, UNITS * TOPK), small(2, UNITS * TOPK)
        top, gx, gsum = small(UNITS, TOPK), small(UNITS, TOPK), small(UNITS)
        efull, gfull = small(UNITS, P), small(UNITS, P)
        eT, gT = small(TOKENS, dt=U32), small(TOKENS)
        iota16 = sb("iota16", [P, TOPK])
        hb = hT[:, :, :].rearrange("p a b -> p (a b)").bitcast(BF16)[:, 0:4 * D].rearrange("p (s d) -> p s d", s=4)
        onesb = sb("onesb", [P, P], BF16)
        wz = sb("wz", [P, 2, 8, 8])
        idx8 = sb("idx8", [P, 2, 8], U32)
        g8, dots, ge = sb("g8", [P, 2, 8]), sb("dots", [P, 2, 8, 2]), sb("ge", [P, 2, 8])
        osb = mmf[:, 0:D]
        hparts = nc.dram_tensor("hparts", (TOKENS, 3, D), BF16, kind="Internal").ap()
        experts = nc.dram_tensor("experts", (TOKENS, D), F32, kind="Internal").ap()

        ln_done, ln_v, ln_a = sem("ln_done"), sem("ln_v"), sem("ln_a")
        att_q, qm_ready, mx_ready, pexp_ready, pn_ready, pt_done, pt_ready, ao_read = (sem(n) for n in (
            "att_q", "qm_ready", "mx_ready", "pexp_ready", "pn_ready", "pt_done", "pt_ready", "ao_read"))
        gate_done, merged_ready, x2_squared = sem("gate_done"), sem("merged_ready"), sem("x2_squared")
        merge_read = [sem(f"merge_read{n}") for n in range(3)]
        out_read = [sem(f"out_read{n}") for n in two]
        turned, turned_read, r3_v, r3_a, in_late, parts_ready, parts_out = (sem(n) for n in (
            "turned", "turned_read", "r3_v", "r3_a", "in_late", "parts_ready", "parts_out"))
        q_read, scores_done, scores_read = ([sem(f"{n}{j}") for j in two] for n in ("q_read", "scores_done", "scores_read"))
        topk_read = [sem(f"topk_read{j}") for j in two]
        soft_in, soft_out, picked, lists_turned, lists_ready = (sem(n) for n in ("soft_in", "soft_out", "picked", "lists_turned", "lists_ready"))
        hb_in, hb_before = (qst_in, qwin_out, sin_in, sin_out), 16 * H
        u_in, v_in = ([sem(f"{n}{s}") for s in range(4)] for n in ("u_in", "v_in"))
        SLOTS = 4
        summed = sem("summed")
        spread, w_ready, ge_ready, idx_ready, g8_ready = sem("spread"), sem("w_ready"), sem("ge_ready"), sem("idx_ready"), sem("g8_ready")
        dotted, acc_read, experts_out = ([sem(f"{n}{s}") for s in two] for n in ("dotted", "acc_read", "experts_out"))
        group = 8
        PAIRS = TOKENS // (2 * group)

        def tile_sum(pe, src, n, bank, count, scaled=ones):
            for kt in range(count):
                last = nc.tensor.matmul(ps[bank][:, 0:n], scaled[:], src[:, kt, 0:n], start=kt == 0, stop=kt == count - 1)
            return last

        block = ctx.enter_context(nc.Block())

        @block.sync
        def _(sp):
            sp.dma_start(mm[:, :, 0:MEM], io["memT"]).then_inc(in_mem, 16)
            sp.dma_start(cst[:], io["consts"]).then_inc(in_cst, 16)

            def load(stage, src, base, i, j):
                n = FIRST[stage] + base + j
                if not isinstance(base, int) or n >= AHEAD:
                    sp.wait_ge(tiles_done, n - AHEAD + 1)
                sp.dma_start(ring[:, j, :], src[base + j]).then_inc(w_in[j], 16)

            for i in range(4):
                for j in range(4):
                    load("kv", io["w_mem"], 4 * i, i, j)
                    if i == 0 and j == 1:
                        sp.dma_start(xT[:, :, :], io["xT"]).then_inc(in_x, 16)
                        sp.dma_start(ab_w[:], io["w_ab"]).then_inc(in_ab, 16)
                        sp.dma_start(rows[:, 0:32], io["dn_rows"].partition_broadcast(P)).then_inc(in_rows, 16)
            with sp.Fori(0, 4) as i:
                for j in range(4):
                    load("glu", io["w_glu"], 4 * i, i, j)
                    if j % 2 == 0:
                        sp.wait_ge(cwin_out[j // 2], 16 * i)
                        sp.wait_ge(conv_read[j // 2], i)
                        sp.dma_start(cwin[:, j // 2, CK - 1 + TP:], io["conv_in"][2 * i + j // 2]).then_inc(cwin_in[j // 2], 16)
            def window_in(h):
                sp.wait_ge(qwin_out, 16 * h)
                sp.wait_ge(qk_ready, h)
                sp.dma_start(qwin[:, :, QWIN0:], io["qkv_in"][h]).then_inc(qst_in, 16)

            def states_in_out(h, store=True):
                if store:
                    sp.wait_ge(state_ready, h)
                    sp.dma_start(io["delta_p"][h - 1], s2).then_inc(s2_out, 16)
                    sp.wait_ge(sn_ready, h)
                    sp.dma_start(io["delta_s"][:, h - 1].rearrange("b d e -> d b e"), sin).then_inc(sin_out, 16)
                    sp.wait_ge(sin_out, 16 * h)
                sp.dma_start(sin, io["delta_in"][:, h].rearrange("b d e -> d b e")).then_inc(sin_in, 16)

            def head_tiles(h, js):
                for j in js:
                    load("head", io["w_head"], 4 * h, h, j)

            window_in(0)
            states_in_out(0, store=False)
            head_tiles(0, range(4))
            head_tiles(1, range(4))
            with sp.Fori(2, H) as h:
                head_tiles(h, range(2))
                window_in(h - 1)
                head_tiles(h, range(2, 4))
                states_in_out(h - 1)
            window_in(H - 1)
            states_in_out(H - 1)
            sp.wait_ge(state_ready, H)
            sp.dma_start(io["delta_p"][H - 1], s2).then_inc(s2_out, 16)
            sp.wait_ge(sn_ready, H)
            sp.dma_start(io["delta_s"][:, H - 1].rearrange("b d e -> d b e"), sin).then_inc(sin_out, 16)
            for a in range(AH):
                for j in range(6):
                    if a == 0 and j == 4:
                        sp.wait_ge(o_done, H)
                        sp.wait_ge(qwin_out, 16 * H)
                    load("att", io["w_att"], 6 * a, a, j)
            with sp.Fori(0, KT) as i:
                for j in range(5):
                    load("merge", io["w_merge"], 5 * i, i, j)
            with sp.Fori(0, 4) as i:
                for j in range(4):
                    load("out", io["w_outp"], 4 * i, i, j)
            sp.wait_ge(out_read[0], 8)
            sp.dma_start(keys[:, :, :], io["keysT"]).then_inc(in_late, 16)
            sp.dma_start(grow, io["g_rows"][0].partition_broadcast(P)).then_inc(in_late, 16)
            with sp.Fori(0, 4) as i:
                for j in range(4):
                    load("pq", io["w_pq"], 4 * i, i, j)
            for t in range(UNITS):
                n = P if t < 2 else NS
                sp.wait_ge(parts_ready, t + 1)
                sp.dma_start(hparts[t * P:t * P + n], parts[0:n, :, :]).then_inc(parts_out, 16)
            sp.wait_ge(parts_out, 48)
            sp.dma_start(grow, io["g_rows"][1].partition_broadcast(P)).then_inc(in_late, 16)
            sp.wait_ge(tiles_done, FIRST["pq"] + 16)
            with sp.Fori(0, PAIRS) as i:
                for r in range(2 * group):
                    s = r % 4
                    sp.wait_ge(spread, 32 * i + 2 * r + 2)
                    sp.dma_start(hb[0:3, s, :], hparts[16 * i + r]).then_inc(hb_in[s], 16)
            for s in two:
                sp.wait_ge(experts_out[s], 16 * PAIRS)
            sp.wait_ge(dotted[1], SLOTS + TOKENS)
            for t in range(UNITS):
                n = P if t < 2 else NS
                sp.dma_start(ring[0:n, t, :], experts[t * P:t * P + n]).then_inc(parts_out, 16)
            for t in range(UNITS):
                n = P if t < 2 else NS
                sp.wait_ge(r3_v, 2 + 3 * (t + 1))
                sp.dma_start(io["y"][t * P:t * P + n], ring[0:n, t, :]).then_inc(in_late, 16)
            sp.wait_ge(in_late, 96)
            sp.wait_ge(stored, 32)
            for s in cwin_out:
                sp.wait_ge(s, 16 * CT // 2)
            sp.wait_ge(qwin_out, 16 * H)
            sp.wait_ge(s2_out, 16 * H)
            sp.wait_ge(sin_out, 16 * H)

        @block.tensor
        def _(pe):
            mat = nc.tensor.matmul

            def arrived(stage, j, i):
                pe.wait_ge(w_in[j], 16 * (BEFORE[stage][j] + 1) + 16 * i)

            def project(bank, j, src, n, kts=KT, k0=0, free=(), close=True):
                for s, count in free:
                    pe.wait_ge(s, count)
                for kt in range(kts):
                    last = mat(ps[bank][:, 0:n], ring[:, j, (k0 + kt) * P:(k0 + kt + 1) * P], src[:, kt, 0:n],
                               start=kt == 0, stop=kt == kts - 1)
                if close:
                    last.then_inc(tiles_done, 1)

            pe.wait_ge(consts_ready, 1)
            for n, (bank, cols) in enumerate(((6, MEM), (7, TOKENS))):
                pe.wait_ge(sq_ready, n + 1)
                tile_sum(pe, hT, cols, bank, KT).then_inc(ss_done, 1)
            pe.wait_ge(norm_ready, 1)
            with pe.Fori(0, 4) as i:
                for j in range(4):
                    arrived("kv", j, i)
                    project(j, j, mm, MEM, free=((kv_free[j], i),))
            for g in range(4):
                pe.wait_ge(kv_free[2 * (g % 2)], 4)
                pe.wait_ge(kv_free[2 * (g % 2) + 1], 4)
                pe.wait_ge(consts_ready, 2)
                if g >= 2:
                    pe.wait_ge(v_placed, g - 1)
                for q in range(4):
                    c, m = 2 * g + q // 2, q % 2
                    last = nc.tensor.transpose(ps[g % 2][:, q * P:(q + 1) * P], vT[:, c, m * P:(m + 1) * P], ident[:])
                last.then_inc(v_turned, 1)
            pe.wait_ge(norm_ready, 2)
            with pe.Fori(0, 4) as i:
                for j in range(4):
                    arrived("glu", j, i)
                    project(4 + j, j, hT, TOKENS, free=((cwin_full[j // 2], i),))
            pe.wait_ge(in_ab, 16)
            pe.wait_ge(v_placed, 4)
            for t in range(UNITS):
                n = P if t < 2 else NS
                for kt in range(KT):
                    last = mat(ps[2][0:n, 32 * t:32 * t + 32], hT[:, kt, t * P:t * P + n], ab_w[:, 32 * kt:32 * kt + 32],
                               start=kt == 0, stop=kt == KT - 1)
            last.then_inc(ab_done, 1)
            pe.wait_ge(ab_ready, 1)
            mat(ps[3][:, 0:32], mu3[:, 0, :], gz[:, 0:32], start=True, stop=True)
            mat(ps[3][:, 32:48], mu3[:, 2, :], gz[:, 32:48], start=True, stop=True)
            mat(ps[3][:, 48:80], ones[:], gz[:, 0:32], start=True, stop=True)
            mat(ps[3][:, 80:96], blk[:], gz[:, 32:48], start=True, stop=True)
            mat(ps[3][:, 96:96 + P], ones[:], gz[:, 48:48 + P], start=True, stop=True).then_inc(sp_b, 1)

            def heads(h, nxt, first=False):
                pieces = []
                if nxt is not None:
                    for j in range(4):
                        for kt in range(KT):
                            pieces.append((j, kt))

                def fill(n):
                    for _ in range(min(n, len(pieces))):
                        j, kt = pieces.pop(0)
                        if kt == 0:
                            arrived("head", j, nxt)
                            pe.wait_ge(proj_read[j], nxt)
                        last = mat(ps[j][:, 0:TOKENS], ring[:, j, kt * P:(kt + 1) * P], hT[:, kt, :],
                                   start=kt == 0, stop=kt == KT - 1)
                        if kt == KT - 1:
                            last.then_inc(tiles_done, 1)

                if first:
                    pe.wait_ge(sp_c, 1)
                    pe.wait_ge(kv_free[3], 4)
                    pe.wait_ge(v_placed, 4)
                    fill(64)
                    return
                h1 = h + 1
                pe.wait_ge(gb_ready, h1)
                pe.wait_ge(o_done, h)
                for u in range(UNITS):
                    mat(ps[7][:, u * P:(u + 1) * P], gb[:, u, :], mu3[:, u, :], start=True, stop=True)
                for u in range(UNITS):
                    last = mat(ps[6][:, u * P:(u + 1) * P], bb[:, u, :], ident[:], start=True, stop=True)
                last.then_inc(rows_done, 1)
                fill(16)
                pe.wait_ge(sq_qk, h1)
                for n in range(2):
                    last = mat(ps[4 + n][:, 0:TOKENS], ones[:], nrm[:, n, :], start=True, stop=True)
                last.then_inc(ssq_done, 1)
                fill(4)
                pe.wait_ge(qk_ready, h1)
                for n, src in enumerate((kn, qn)):
                    for u in range(UNITS):
                        c = slice(u * P, (u + 1) * P)
                        last = mat(ps[4 + n][:, c], kn[:, c], src[:, c], start=True, stop=True)
                last.then_inc(g_done, 1)
                pe.wait_ge(rows_used, 2 * h1)
                pe.wait_ge(v_ready, h1)
                for bank, src in ((6, kn), (7, vv)):
                    for u in range(UNITS):
                        last = nc.tensor.transpose(ps[bank][:, u * P:(u + 1) * P], src[:, u * P:(u + 1) * P], ident[:])
                last.then_inc(tok_done, 1)
                pe.wait_ge(knm_ready, h1)
                pe.wait_ge(sin_in, 16 * h1)
                pe.wait_ge(tok_read, 2 * h1)
                for b in range(NBATCH):
                    last = mat(ps[7][0:NS, 384:512], knm[:, b * NS:(b + 1) * NS], sin[:, b, :], start=b == 0, stop=b == NBATCH - 1)
                last.then_inc(ks_done, 1)
                fill(4)
                pe.wait_ge(t_ready, T_STEPS * h + 1)
                for u in range(UNITS):
                    last = nc.tensor.transpose(ps[4][:, u * P:(u + 1) * P], tt[:, u, :], ident[:])
                last.then_inc(turn_done, 1)
                fill(3)
                for l in range(1, len(LEVELS)):
                    units = UNITS if l < SAMPLE_LEVELS else 2
                    pe.wait_ge(t_ready, T_STEPS * h + 2 * l)
                    pe.wait_ge(lt_ready, len(LEVELS) * h + l + 1)
                    for u in range(units):
                        last = mat(ps[4][:, u * P:(u + 1) * P], lt[:, l, u * P:(u + 1) * P], tn[:, u, :], start=True, stop=True)
                    last.then_inc(p_done, 1)
                    fill(2)
                    pe.wait_ge(p_ready, 6 * h + l)
                    if l < len(LEVELS) - 1:
                        for u in range(units):
                            last = mat(ps[5][:, u * P:(u + 1) * P], tt[:, u, :], pm[:, u, :], start=True, stop=True)
                        last.then_inc(dd_done, 1)
                    for u in range(units):
                        last = mat(ps[6][:, u * P:(u + 1) * P], pm[:, u, :], tt[:, u, :], start=True, stop=True)
                    last.then_inc(dd_done, 1)
                    fill(3)
                pe.wait_ge(t_ready, T_STEPS * h + T_STEPS)
                pe.wait_ge(r_ready, 2 * h + 1)
                mat(ps[7][:, 0:P], tt[:, 0, :], vb[:, 0, :], start=True, stop=True)
                mat(ps[7][:, P:2 * P], tt[:, 2, :], vb[:, 2, :], start=True, stop=True).then_inc(u_done, 1)
                fill(3)
                pe.wait_ge(u_ready, 2 * h + 1)
                mat(ps[4][:, 0:P], kd[:, 0, :], uu[:, 0, :], start=True, stop=True).then_inc(s_done, 1)
                mat(ps[5][:, 0:P], uu[:, 0, :], qkd[:, 0, :], start=True, stop=True)
                pe.wait_ge(qd_ready, h1)
                mat(ps[5][:, 256:TOKENS], uu[:, 1, :], qkd[:, 2, 0:NS], start=True, stop=False, skip_group_check=True)
                for b in range(NBATCH):
                    c = slice(TP + b * TS, TP + (b + 1) * TS)
                    mat(ps[5][:, c], sin[:, b, :], qn[:, c], start=False, stop=b == NBATCH - 1, skip_group_check=True)
                pe.wait_ge(s1_ready, h1)
                mat(ps[7][:, 2 * P:3 * P], kn[:, P:2 * P], s1, start=True, stop=True).then_inc(ks_done, 1)
                pe.wait_ge(um_ready, h1)
                umf = um.rearrange("p b e -> p (b e)")
                mat(ps[6][:, :], kd[:, 2, :], umf[:, 0:512], start=True, stop=True).then_inc(sn_done, 1)
                pe.wait_ge(r_ready, 2 * h + 2)
                mat(ps[7][:, 0:P], tt[:, 1, :], vb[:, 1, :], start=True, stop=True).then_inc(u_done, 1)
                fill(2)
                pe.wait_ge(u_ready, 2 * h + 2)
                mat(ps[5][:, P:2 * P], uu[:, 2, :], qkd[:, 1, :], start=True, stop=False)
                mat(ps[5][:, P:2 * P], s1, qn[:, P:2 * P], start=False, stop=True)
                mat(ps[4][:, P:2 * P], kd[:, 1, :], uu[:, 2, :], start=True, stop=True).then_inc(so_done, 1)
                mat(ps[7][:, :], kd[:, 2, :], umf[:, 512:1024], start=True, stop=True).then_inc(sn_done, 1)
                fill(2)
                pe.wait_ge(osq_ready, h1)
                pe.wait_ge(state_ready, h1)
                mat(ps[4][:, 0:TOKENS], ones[:], sqo, start=True, stop=True).then_inc(oss_done, 1)
                fill(64)

            heads(None, 0, first=True)
            with pe.Fori(0, H - 1) as h:
                heads(h, h + 1)
            heads(H - 1, None)
            pe.wait_ge(o_done, H)
            for q in two:
                pe.wait_ge(conv_read[q], 4)
            tile_sum(pe, cT, TOKENS, 4, CT).then_inc(ln_done, 1)
            for a in range(AH):
                done = FIRST["att"] + 6 * a
                for j in range(2):
                    arrived("att", j, a)
                    project(j, j, hT, TOKENS, free=((att_q, 2 * a),) if a else ())
                if a == 0:
                    pe.wait_ge(ln_a, 1)
                    tile_sum(pe, lnsq, TOKENS, 5, CT).then_inc(ln_done, 1)
                pe.wait_ge(att_q, 2 * a + 2)
                pe.wait_ge(qm_ready, a + 1)
                for t in two:
                    for d in two:
                        mat(ps[2][:, t * MEM:(t + 1) * MEM], xq[:, d, t * P:(t + 1) * P], kmem[:, 2 * a + d, :], start=d == 0, stop=d == 1)
                arrived("att", 2, a)
                arrived("att", 3, a)
                for b in range(NBATCH):
                    for d in two:
                        at_ = (b % 4) * 512 + d * MEM
                        last = mat(ps[3][0:NS, 0:MEM], qm[:, d, b * NS:(b + 1) * NS], ring[:, 2 + b // 4, at_:at_ + MEM],
                                   start=b + d == 0, stop=b == NBATCH - 1 and d == 1)
                    if b % 4 == 3:
                        last.then_inc(tiles_done, 1)
                pe.wait_ge(pn_ready, a + 1)
                for m in two:
                    for t in two:
                        nc.tensor.transpose(ps[6][:, m * MEM + t * P:m * MEM + (t + 1) * P], pp[:, t, m * P:(m + 1) * P], ident[:])
                    last = nc.tensor.transpose(ps[7][:, m * NS:(m + 1) * NS], pp[0:NS, 2, m * P:(m + 1) * P], ident[0:NS, 0:NS])
                last.then_inc(pt_done, 1)
                pe.wait_ge(pt_ready, 2 * a + 2)
                pe.wait_ge(ln_v, 2)
                arrived("att", 4, a)
                arrived("att", 5, a)
                if a:
                    pe.wait_ge(ao_read, a)
                for d in two:
                    at_ = a * 256 + d * P
                    for m in two:
                        mat(ps[4 + d][:, 0:TP], vmem[:, m, at_:at_ + P], pT[:, m, 0:TP], start=m == 0, stop=m == 1)
                for b in range(NBATCH):
                    c = slice(TP + b * TS, TP + (b + 1) * TS)
                    for d in two:
                        for m in two:
                            at_ = (b % 4) * 512 + m * 256 + d * P
                            last = mat(ps[4 + d][:, c], ring[:, 4 + b // 4, at_:at_ + P], pT[:, m, c], start=m == 0, stop=m == 1)
                    if b % 4 == 3:
                        last.then_inc(tiles_done, 1)
            pe.wait_ge(ln_v, 4)
            pe.wait_ge(ao_read, AH)
            with pe.Fori(0, KT) as i:
                arrived("merge", 0, i)
                project(0, 0, hT, TOKENS, free=((merge_read[0], i),))
                arrived("merge", 1, i)
                project(1, 1, cT, TOKENS, kts=CT, close=False)
                project(5, 1, xoT, TOKENS, kts=CT, k0=CT, free=((merge_read[2], i),))
                arrived("merge", 2, i)
                project(2, 2, hT, TOKENS, free=((merge_read[1], i),))
                arrived("merge", 3, i)
                project(3, 3, oT, TOKENS)
                arrived("merge", 4, i)
                project(4, 4, hT, TOKENS)
            pe.wait_ge(merged_ready, KT)
            with pe.Fori(0, 4) as i:
                for j in range(4):
                    arrived("out", j, i)
                    project(6 + j % 2, j, mm, TOKENS, free=((out_read[j % 2], 2 * i + j // 2),))
            pe.wait_ge(x2_squared, KT)
            tile_sum(pe, hT, TOKENS, 5, KT).then_inc(ss_done, 1)
            for t in range(UNITS):
                n = P if t < 2 else NS
                for q in range(4):
                    if 4 * t + q >= 4:
                        pe.wait_ge(turned_read, 4 * t + q - 3)
                    for kt in range(4):
                        last = nc.tensor.transpose(ps[q][0:n, kt * P:(kt + 1) * P], xT[:, 4 * q + kt, t * P:t * P + n], ident[:])
                    last.then_inc(turned, 1)
            pe.wait_ge(norm_ready, 3)
            pe.wait_ge(in_late, 32)
            with pe.Fori(0, 4) as i:
                for j in range(4):
                    b, n = j % 2, 2 * i + j // 2
                    arrived("pq", j, i)
                    project(4 + b, j, hT, TOKENS, free=((q_read[b], n),))
                    pe.wait_ge(q_read[b], n + 1)
                    pe.wait_ge(scores_read[b], n)
                    for t in range(UNITS):
                        w = P if t < 2 else NS
                        last = mat(ps[6 + b][0:w, t * P:(t + 1) * P], qs[:, b, t * P:t * P + w], keys[:, j % 2, :], start=True, stop=True)
                    last.then_inc(scores_done[b], 1)
            pe.wait_ge(picked, PH)
            for n, src in enumerate((efull, gfull)):
                for t in range(UNITS):
                    w = P if t < 2 else NS
                    last = nc.tensor.transpose(ps[n][:, t * P:t * P + w], src[0:w, t, :], ident[0:w, 0:w])
                    if n == 0 and t < 2:
                        last.then_inc(*((spread, 2 * SLOTS) if t else (summed, SLOTS)))
            last.then_inc(lists_turned, 1)
            def spread_token(i, r):
                s = r % 4
                pe.wait_ge(hb_in[s], 64 * i + 16 * (r // 4) + 16 + hb_before)
                for half_ in two:
                    pe.wait_ge(dotted[half_], 16 * i + r + SLOTS)
                    for q in (2 * half_, 2 * half_ + 1):
                        last = mat(ps[q][:, :], onesb[0:3, :], hb[0:3, s, q * 512:(q + 1) * 512], start=True, stop=True)
                    last.then_inc(spread, 1)

            def pair(i, final=False):
                for r in range(2 * group):
                    s, g_ = r % 4, r // group
                    if r < 2 * group - 1:
                        spread_token(i, r + 1)
                    elif not final:
                        spread_token(i + 1, 0)
                    pe.wait_ge(w_ready, 16 * i + r + 1)
                    pe.wait_ge(v_in[s], 64 * i + 16 * (r // 4) + 16)
                    if r % group == 0:
                        pe.wait_ge(acc_read[g_], i)
                    for q in range(4):
                        last = mat(psum[32 * g_:32 * g_ + group, 4 + q, :], wz[:, g_, r % group, :], ring[:, 4 + s, q * 512:(q + 1) * 512],
                                   start=r % group == 0, stop=r % group == group - 1, skip_group_check=True)
                    last.then_inc(summed, 1)

            pe.wait_ge(lists_ready, 2)
            spread_token(0, 0)
            with pe.Fori(0, PAIRS - 1) as i:
                pair(i)
            pair(PAIRS - 1, final=True)

        @block.scalar
        def _(act):
            fn = nc.scalar.activation

            def rooted(n, cols, buf=None):
                act.wait_ge(ms_ready, n)
                fn(rs[:, 0:cols], rs[:, 0:cols], ACT.Sqrt).then_inc(rt_ready, 1)

            act.wait_ge(in_mem, 16)
            fn(hT[:, :, 0:MEM], mm[:, :, 0:MEM], ACT.Square).then_inc(sq_ready, 1)
            rooted(1, MEM)
            act.wait_ge(in_x, 16)
            act.wait_ge(ss_done, 1)
            fn(hT[:, :, :], xT[:, :, :], ACT.Square).then_inc(sq_ready, 1)
            rooted(2, TOKENS)
            with act.Fori(0, 2) as i:
                for j in range(4):
                    act.wait_ge(tiles_done, 4 * i + j + 1)
                    fn(kmem[:, 4 * i + j, :], ps[j][:, 0:MEM], ACT.Copy).then_inc(kv_free[j], 1)
            with act.Fori(0, 2) as i:
                for j in range(4):
                    act.wait_ge(tiles_done, 4 * i + j + 9)
                    fn(vT[:, 4 * i + j, :], ps[j][:, 0:MEM], ACT.Copy).then_inc(kv_free[j], 1)
            for j in range(4):
                act.wait_ge(kv_free[j], 4)
            act.dma_start(io["mem_k"], kmem[:, :, :]).then_inc(stored, 16)
            act.wait_ge(v_placed, 4)
            act.dma_start(io["mem_v"], vmem[:, :, :]).then_inc(stored, 16)
            with act.Fori(0, 4) as i:
                for q in range(2):
                    act.wait_ge(tiles_done, FIRST["glu"] + 4 * i + 2 * q + 2)
                    act.wait_ge(conv_read[q], i)
                    fn(sg[:, q, :], ps[5 + 2 * q][:, 0:TOKENS], ACT.Tanh, scale=0.5).then_inc(gate_ready[q], 1)
                    act.wait_ge(cwin_full[q], i + 1)
                    act.dma_start(io["conv_out"][2 * i + q], cwin[:, q, :]).then_inc(cwin_out[q], 16)
            act.wait_ge(ab_done, 1)
            for u in range(UNITS):
                n = P if u < 2 else NS
                last = fn(ab[0:n, u, :], ps[2][0:n, 32 * u:32 * u + 32], ACT.Copy)
            last.then_inc(sp_a, 1)
            act.wait_ge(sp_v, 1)
            fn(sp3[:, 1, :], sp3[:, 0, :], ACT.Exp, scale=-1.0).then_inc(sp_s, 1)
            fn(rows[:, 0:16], rows[:, 0:16], ACT.Exp).then_inc(sp_s, 1)
            act.wait_ge(sp_v, 2)
            fn(sp3[:, 1, :], sp3[:, 1, :], ACT.Ln).then_inc(sp_s, 1)
            fn(sp3[:, 3, :], sp3[:, 3, :], ACT.Tanh, scale=0.5).then_inc(sp_s, 1)
            act.wait_ge(sp_v, 3)
            fn(ex[:], ex[:], ACT.Exp).then_inc(sp_s, 1)

            act.wait_ge(sp_c, 2)
            with act.Fori(0, H) as h:
                h1 = h + 1
                act.wait_ge(qst_in, 16 * h1)
                for j in range(3):
                    act.wait_ge(tiles_done, FIRST["head"] + 4 * h + j + 1)
                    fn(qwin[:, j, QK - 1:QWIN0], ps[j][:, 0:TP], ACT.Copy)
                    fn(qwin[:, j, QWIN0:].rearrange("p (b s) -> p b s", b=NBATCH)[:, :, QK - 1:],
                       ps[j][:, TP:TOKENS].rearrange("p (b s) -> p b s", b=NBATCH), ACT.Copy).then_inc(proj_read[j], 1)
                act.wait_ge(tiles_done, FIRST["head"] + 4 * h + 4)
                act.wait_ge(o_done, h)
                fn(zs, ps[3][:, 0:TOKENS], ACT.Tanh, scale=0.5).then_inc(z_ready, 1)
                for j in range(3):
                    act.wait_ge(proj_read[j], h1)
                act.dma_start(io["qkv_out"][h], qwin[:, :, :]).then_inc(qwin_out, 16)
                for j in range(3):
                    act.wait_ge(conv_ready, 3 * h + j + 1)
                    fn(th[:, j, :], cv[:, j, :], ACT.Tanh).then_inc(tanh_ready, 1)
                act.wait_ge(dt_ready, h1)
                fn(egb[:], ps[7][:, 0:UT], ACT.Exp).then_inc(rows_used, 1)
                fn(dt3[:, :, :], dt3[:, :, :], ACT.Exp).then_inc(dtx_ready, 1)
                act.wait_ge(silu_ready, 2 * h1)
                fn(nrm[:, :, :], cv[:, 0:2, :], ACT.Square).then_inc(sq_qk, 1)
                act.wait_ge(nrm_ready, h1)
                fn(nrm[:, :, :], nrm[:, :, :], ACT.Sqrt).then_inc(nrt_ready, 1)
                act.wait_ge(tok_done, h1)
                for u in range(UNITS):
                    last = fn(kd[:, u, :], ps[6][:, u * P:(u + 1) * P], ACT.Copy, scale=hs[:, KDEC + u:KDEC + u + 1])
                last.then_inc(tok_read, 1)
                for u in range(UNITS):
                    last = fn(vb[:, u, :], ps[7][:, u * P:(u + 1) * P], ACT.Copy, scale=hs[:, BETA + u:BETA + u + 1])
                last.then_inc(tok_read, 1)
                for l in range(1, len(LEVELS)):
                    units = UNITS if l < SAMPLE_LEVELS else 2
                    act.wait_ge(p_done, 6 * h + l)
                    fn(pm[:, 0:units, :], three(4)[:, 0:units, :], ACT.Copy).then_inc(p_ready, 1)
                act.wait_ge(u_done, 2 * h + 1)
                fn(uu[:, 0:2, :], three(7)[:, 0:2, :], ACT.Copy).then_inc(u_ready, 1)
                act.wait_ge(s_done, h1)
                act.wait_ge(s2_out, 16 * h)
                fn(s1, ps[4][:, 0:P], ACT.Copy).then_inc(s1_ready, 1)
                act.wait_ge(u_done, 2 * h + 2)
                fn(uu[:, 2, :], ps[7][:, 0:P], ACT.Copy).then_inc(u_ready, 1)
                act.wait_ge(so_done, h1)
                fn(sqo, ps[5][:, 0:TOKENS], ACT.Square).then_inc(osq_ready, 1)
                act.wait_ge(orm_ready, h1)
                fn(rs[:], rs[:], ACT.Sqrt).then_inc(ort_ready, 1)
            act.wait_ge(ln_v, 1)
            fn(lnsq, cT, ACT.Square).then_inc(ln_a, 1)
            act.wait_ge(sin_out, 16 * H)
            for a in range(AH):
                done = FIRST["att"] + 6 * a
                for d in two:
                    act.wait_ge(tiles_done, done + d + 1)
                    fn(xq[:, d, :], ps[d][:, 0:TOKENS], ACT.Copy).then_inc(att_q, 1)
                if a == 0:
                    act.wait_ge(ln_v, 2)
                    fn(rs[:], rs[:], ACT.Sqrt).then_inc(ln_a, 1)
                    act.wait_ge(ln_v, 3)
                    fn(lnsq, cT, ACT.Tanh).then_inc(ln_a, 1)
                act.wait_ge(mx_ready, a + 1)
                for t in range(UNITS):
                    n = P if t < 2 else NS
                    src = ps[2][:, t * MEM:(t + 1) * MEM] if t < 2 else ps[3][0:n, 0:MEM]
                    last = fn(pp[0:n, t, :], src, ACT.Exp, bias=mx[0:n, t:t + 1], scale=1.0 / 16.0, accum_out=sm[0:n, t:t + 1])
                last.then_inc(pexp_ready, 1)
                act.wait_ge(pt_done, a + 1)
                fn(pT[:, :, 0:TP], ps[6].rearrange("p (m t) -> p m t", m=2), ACT.Copy).then_inc(pt_ready, 1)
            with act.Fori(0, KT) as i:
                for n in range(3):
                    act.wait_ge(tiles_done, FIRST["merge"] + 5 * i + 2 * n + 1)
                    act.wait_ge(merge_read[n], i)
                    fn(g3[:, n, :], ps[2 * n][:, 0:TOKENS], ACT.Tanh, scale=0.5).then_inc(gate_done, 1)
            with act.Fori(0, 4) as i:
                for j in range(4):
                    act.wait_ge(out_read[j % 2], 2 * i + j // 2 + 1)
                    fn(hT[:, 4 * i + j, :], xT[:, 4 * i + j, :], ACT.Square).then_inc(x2_squared, 1)
            rooted(3, TOKENS)
            for t in range(UNITS):
                n = P if t < 2 else NS
                for q in range(4):
                    act.wait_ge(turned, 4 * t + q + 1)
                    fn(x2tok[0:n, t, q * 512:(q + 1) * 512], ps[q][0:n, :], ACT.Copy).then_inc(turned_read, 1)
            act.wait_ge(turned_read, 12)
            for t in range(UNITS):
                n = P if t < 2 else NS
                last = fn(seven[0:n, :], x2tok[0:n, t, :], ACT.Square, accum_out=r3[0:n, t:t + 1])
                last.then_inc(r3_a, 1)
                act.wait_ge(r3_a, t + 1)
            act.wait_ge(r3_v, 1)
            fn(r3[:], r3[:], ACT.Sqrt).then_inc(r3_a, 1)
            with act.Fori(0, 4) as i:
                def take(j):
                    b, n = j % 2, 2 * i + j // 2
                    act.wait_ge(scores_done[b], n + 1)
                    act.wait_ge(topk_read[j // 2], i)
                    for t in range(UNITS):
                        w = P if t < 2 else NS
                        last = fn(sc[0:w, j, t * P:(t + 1) * P], ps[6 + b][0:w, t * P:(t + 1) * P], ACT.Copy)
                    last.then_inc(scores_read[b], 1)

                def soften(q):
                    act.wait_ge(soft_in, 2 * i + q + 1)
                    fn(gx[:, :, :], gx[:, :, :], ACT.Exp).then_inc(soft_out, 1)

                for j in range(4):
                    b, n = j % 2, 2 * i + j // 2
                    act.wait_ge(tiles_done, FIRST["pq"] + 4 * i + j + 1)
                    act.wait_ge(scores_done[b], n)
                    fn(qs[:, b, :], ps[4 + b][:, 0:TOKENS], ACT.Copy).then_inc(q_read[b], 1)
                    take(j)
                    if j == 3:
                        soften(0)
                soften(1)
            def weigh(i, r):
                g_, j = r // group, r % group
                n = 16 * i + r
                act.wait_ge(dotted[1], n + 1 + SLOTS)
                fn(ge[:, g_, j:j + 1], dots[:, g_, j, 0:1], ACT.Gelu_apprx_tanh, bias=dots[:, g_, j, 1:2]).then_inc(ge_ready, 1)
                act.wait_ge(ge_ready, n + 1)
                fn(wz[:, g_, j, j:j + 1], ge[:, g_, j:j + 1], ACT.Copy, scale=g8[:, g_, j:j + 1]).then_inc(w_ready, 1)

            def store_group(i, g_):
                act.wait_ge(summed, 16 * i + group * (g_ + 1) + SLOTS)
                act.wait_ge(experts_out[g_], 16 * i)
                fn(osb[32 * g_:32 * g_ + group, :].rearrange("p (q n) -> p q n", q=4), psum[32 * g_:32 * g_ + group, 4:8, :], ACT.Copy)\
                    .then_inc(acc_read[g_], 1)
                act.wait_ge(acc_read[g_], i + 1)
                act.dma_start(experts[bass.ds(16 * i + 8 * g_, group)], osb[32 * g_:32 * g_ + group, :]).then_inc(experts_out[g_], 16)

            def act_pair(i, first=False):
                for g_ in two:
                    if not first or g_:
                        act.wait_ge(w_ready, 16 * i + 8 * g_)
                    fn(g8[:, g_, :], gT[:, bass.ds(16 * i + 8 * g_, group)] if not first else gT[:, 8 * g_:8 * g_ + 8], ACT.Copy)\
                        .then_inc(g8_ready, 1)
                    act.wait_ge(g8_ready, 2 * i + g_ + 1)
                    for j in range(group):
                        weigh(i, group * g_ + j)
                        if j == 1:
                            if g_:
                                store_group(i, 0)
                            elif not first:
                                store_group(i - 1, 1)

            act.wait_ge(lists_ready, 2)
            act_pair(0, first=True)
            with act.Fori(1, PAIRS) as i:
                act_pair(i)
            store_group(PAIRS - 1, 1)
            for t in range(UNITS):
                n = P if t < 2 else NS
                act.wait_ge(r3_v, 2 + 1 + 3 * t)
                fn(ring[0:n, 4 + t, :], ring[0:n, t, :], ACT.Square, accum_out=r3[0:n, t:t + 1]).then_inc(r3_a, 1)
                act.wait_ge(r3_v, 2 + 2 + 3 * t)
                fn(r3[0:n, t:t + 1], r3[0:n, t:t + 1], ACT.Sqrt).then_inc(r3_a, 1)

        @block.vector
        def _(dve):
            v = nc.vector
            st = Steps(dve, dve_step)

            def finish_norm(n, src, dst, gains, cols, bank, width):
                dve.wait_ge(ss_done, n)
                v.tensor_scalar(rs[:, 0:cols], ps[bank][:, 0:cols], 1.0 / width, EPS, ALU.mult, ALU.add).then_inc(ms_ready, 1)
                dve.wait_ge(rt_ready, n)
                st(v.reciprocal(rs[:, 0:cols], rs[:, 0:cols]))
                st.wait()
                for kt in range(KT):
                    last = v.scalar_tensor_tensor(dst[:, kt, 0:cols], src[:, kt, 0:cols], cst[:, gains + kt:gains + kt + 1],
                                                  rs[:, 0:cols], ALU.mult, ALU.mult)
                last.then_inc(norm_ready, 1)

            st(v.memset(ab[:, :, :], 0.0))
            st(v.memset(cwin[:, :, 0:CK - 1], 0.0))
            dve.wait_ge(in_cst, 16)
            finish_norm(1, mm, mm, C_MEM, MEM, 6, D)
            dve.wait_ge(norm_ready, 1)
            finish_norm(2, xT, hT, C_MIX, TOKENS, 7, D)
            st(v.tensor_scalar(half[:, 0:CT], cst[:, C_LNB:C_LNB + CT], 0.5, None, ALU.mult))
            st(v.tensor_scalar(half[:, CT:CT + 1], cst[:, C_DNG:C_DNG + 1], 0.5, None, ALU.mult))
            for g in range(4):
                dve.wait_ge(v_turned, g + 1)
                for q in range(4):
                    c, m = 2 * g + q // 2, q % 2
                    last = v.tensor_copy(vmem[:, m, c * P:(c + 1) * P], ps[g % 2][:, q * P:(q + 1) * P])
                last.then_inc(v_placed, 1)
            with dve.Fori(0, 4) as i:
                st.enter(i, 2 * (2 * CK + 2))
                for q in range(2):
                    c = 2 * i + q
                    dve.wait_ge(gate_ready[q], i + 1)
                    st(v.tensor_scalar(sg[:, q, :], sg[:, q, :], 0.5, 0.5, ALU.mult, ALU.add))
                    dwp = dwp2[:, q, :]
                    dve.wait_ge(conv_read[q], i)
                    st(v.tensor_copy(dwp[:, 0:CK], cst[:, bass.ds(C_DW + c * CK, CK)]))
                    st(v.tensor_copy(dwp[:, CK:CK + 1], cst[:, bass.ds(C_DWB + c, 1)]))
                    st.wait()
                    prompt = cwin[:, q, 0:CK - 1 + TP]
                    sample = cwin[:, q, CK - 1 + TP:].rearrange("p (b s) -> p b s", b=NBATCH)
                    v.tensor_tensor(prompt[:, CK - 1:], ps[4 + 2 * q][:, 0:TP], sg[:, q, 0:TP], ALU.mult)
                    dve.wait_ge(cwin_in[q], 16 * i + 16)
                    v.tensor_tensor(sample[:, :, CK - 1:], ps[4 + 2 * q][:, TP:TOKENS].rearrange("p (b s) -> p b s", b=NBATCH),
                                    sg[:, q, TP:].rearrange("p (b s) -> p b s", b=NBATCH), ALU.mult).then_inc(cwin_full[q], 1)
                    dve.wait_ge(cwin_full[q], i + 1)
                    out_p = cT[:, c, 0:TP]
                    out_s = cT[:, c, TP:TOKENS].rearrange("p (b s) -> p b s", b=NBATCH)
                    acc_p, acc_s = sg[:, q, 0:TP], sg[:, q, TP:].rearrange("p (b s) -> p b s", b=NBATCH)
                    for t in range(CK):
                        w = dwp[:, t:t + 1]
                        last_tap = t == CK - 1
                        for src, acc_, out_ in ((prompt[:, t:t + TP], acc_p, out_p), (sample[:, :, t:t + TS], acc_s, out_s)):
                            if t == 0:
                                ins = v.tensor_scalar(acc_, src, w, dwp[:, CK:CK + 1], ALU.mult, ALU.add)
                            else:
                                st.wait(st.n - 1)
                                ins = v.scalar_tensor_tensor(out_ if last_tap else acc_, src, w, acc_, ALU.mult, ALU.add)
                            if last_tap and acc_ is acc_s:
                                ins.then_inc(conv_read[q], 1)
                            else:
                                st(ins)
                st.leave(4)
            def uh(x):
                return x.rearrange("p (u h) -> p u h", u=UNITS)

            def hu(at_, n=UNITS):
                return hp[:, :, at_:at_ + n].rearrange("p h u -> p u h")

            raw, beta = uh(sp3[:, 2, :]), uh(sp3[:, 3, :])
            dve.wait_ge(in_rows, 16)
            dve.wait_ge(sp_a, 1)
            dt_row = rows[:, 16:32].unsqueeze(1).to_broadcast([P, UNITS, 16])
            st(v.tensor_tensor(raw, ab[:, :, 0:16], dt_row, ALU.add))
            v.tensor_copy(beta, ab[:, :, 16:32])
            st.wait()
            st(v.tensor_scalar(sp3[:, 1, :], sp3[:, 2, :], -1.0, None, ALU.mult))
            st.wait()
            st(v.tensor_tensor(sp3[:, 0, :], sp3[:, 1, :], sp3[:, 2, :], ALU.max))
            v.tensor_scalar(sp3[:, 2, :], sp3[:, 2, :], 0.0, None, ALU.max).then_inc(sp_v, 1)
            dve.wait_ge(sp_s, 2)
            v.tensor_scalar(sp3[:, 1, :], sp3[:, 1, :], 1.0, None, ALU.add).then_inc(sp_v, 1)
            dve.wait_ge(sp_s, 4)
            st(v.tensor_tensor(sp3[:, 2, :], sp3[:, 2, :], sp3[:, 1, :], ALU.add))
            st(v.tensor_scalar(sp3[:, 3, :], sp3[:, 3, :], 0.5, 0.5, ALU.mult, ALU.add))
            st.wait()
            st(v.scalar_tensor_tensor(uh(gz[:, 0:48]), raw, -1.0, rows[:, 0:16].unsqueeze(1).to_broadcast([P, UNITS, 16]),
                                      ALU.mult, ALU.mult))
            st.wait()
            st(v.memset(gz[NS:P, 32:48], 0.0))
            st.wait()
            v.tensor_tensor(gz[:, 48:].rearrange("p (b h) -> p b h", b=NBATCH),
                            gz[:, 32:48].unsqueeze(1).to_broadcast([P, NBATCH, H]),
                            bm[:].unsqueeze(2).to_broadcast([P, NBATCH, H]), ALU.mult).then_inc(ab_ready, 1)
            dve.wait_ge(sp_b, 1)
            st(v.tensor_copy(ex[:, 0:48], ps[3][:, 0:48]))
            st.wait()
            v.tensor_copy(ex[:, 96:144], ps[3][:, 48:96])
            v.tensor_copy(ex[:, 144:], ps[3][:, 96:96 + P])
            v.tensor_tensor(ex[:, 48:96], ps[3][:, 48:96], ex[:, 0:48], ALU.subtract)
            v.tensor_copy(hu(GC), uh(ps[3][:, 0:48])).then_inc(sp_v, 1)
            v.tensor_copy(hu(BETA), beta)
            v.tensor_copy(hu(GRAW), uh(gz[:, 0:48]))
            for pad in (qn, kn, vv):
                v.memset(pad[:, TOKENS:], 0.0)
            v.memset(knm, 0.0)
            dve.wait_ge(sp_s, 5)
            v.scalar_tensor_tensor(hu(NBEG), uh(ex[:, 0:48]), -1.0, beta, ALU.mult, ALU.mult)
            v.tensor_copy(hu(KDEC), uh(ex[:, 48:96]))
            v.tensor_copy(hu(EGL, 2), uh(ex[:, 96:144])[:, 0:2, :])
            v.tensor_copy(hu(EGLB, NBATCH), ex[:, 144:].rearrange("p (b h) -> p b h", b=NBATCH)).then_inc(sp_c, 1)
            v.memset(qwin[:, :, 0:QK - 1], 0.0).then_inc(sp_c, 1)
            dve.wait_ge(sp_c, 2)

            with dve.Fori(0, H) as h:
                h1 = h + 1
                st.enter(h, HEAD_STEPS)
                v.tensor_copy(hs[:], hp[:, h, :])
                st(v.tensor_scalar(pw[:], cst[:, bass.ds(C_DNW + h * 3 * QK, 3 * QK)], 0.5, None, ALU.mult))
                st.wait()
                for j in range(3):
                    dve.wait_ge(proj_read[j], h1)
                    prompt = qwin[:, j, 0:QWIN0]
                    sample = qwin[:, j, QWIN0:].rearrange("p (b s) -> p b s", b=NBATCH)
                    acc_p, acc_s = cv[:, j, 0:TP], cv[:, j, TP:].rearrange("p (b s) -> p b s", b=NBATCH)
                    for t in range(QK):
                        w = pw[:, j * QK + t:j * QK + t + 1]
                        for src, acc_ in ((prompt[:, t:t + TP], acc_p), (sample[:, :, t:t + TS], acc_s)):
                            if t == 0:
                                ins = v.tensor_scalar(acc_, src, w, None, ALU.mult)
                            else:
                                st.wait(st.n - 1)
                                ins = v.scalar_tensor_tensor(acc_, src, w, acc_, ALU.mult, ALU.add)
                            if t == QK - 1 and acc_ is acc_s:
                                ins.then_inc(conv_ready, 1)
                            else:
                                st(ins)
                dve.wait_ge(z_ready, h1)
                v.scalar_tensor_tensor(zs, zs, 1.0, ps[3][:, 0:TOKENS], ALU.add, ALU.mult).then_inc(proj_read[3], 1)
                dve.wait_ge(rows_done, h1)
                for u in range(UNITS):
                    last = v.tensor_scalar(dt3[:, u, :], ps[7][:, u * P:(u + 1) * P], hs[:, GC + u:GC + u + 1], 0.0,
                                           ALU.subtract, ALU.min)
                last.then_inc(dt_ready, 1)
                for j in range(3):
                    dve.wait_ge(tanh_ready, 3 * h + j + 1)
                    out_ = cv[:, j, :] if j < 2 else vv[:, 0:TOKENS]
                    v.scalar_tensor_tensor(out_, th[:, j, :], 1.0, cv[:, j, :], ALU.add, ALU.mult)\
                        .then_inc(silu_ready if j < 2 else v_ready, 1)
                dve.wait_ge(dtx_ready, h1)
                st(v.tensor_tensor(dt3[:, :, :], dt3[:, :, :], mu3[:, :, :], ALU.mult))
                st.wait()
                st(v.tensor_tensor(db3[:, :, :], dt3[:, :, :], three(6), ALU.mult))
                st.wait()
                dve.wait_ge(ssq_done, h1)
                v.tensor_scalar(nrm[:, 0, :], ps[4][:, 0:TOKENS], EPS, None, ALU.add).then_inc(rows_used, 1)
                v.tensor_scalar(nrm[:, 1, :], ps[5][:, 0:TOKENS], EPS, None, ALU.add).then_inc(nrm_ready, 1)
                dve.wait_ge(nrt_ready, h1)
                st(v.reciprocal(nrm[:, :, :], nrm[:, :, :]))
                st.wait()
                st(v.tensor_tensor(kn[:, 0:TOKENS], cv[:, 1, :], nrm[:, 1, :], ALU.mult))
                v.scalar_tensor_tensor(qn[:, 0:TOKENS], cv[:, 0, :], float(P) ** -0.5, nrm[:, 0, :], ALU.mult, ALU.mult)\
                    .then_inc(qk_ready, 1)
                st.wait()
                v.tensor_copy(knm.rearrange("p (b s) -> p b s", s=72)[:, :, 0:TS],
                              kn[:, TP:TOKENS].rearrange("p (b s) -> p b s", b=NBATCH)).then_inc(knm_ready, 1)
                dve.wait_ge(g_done, h1)
                v.tensor_tensor(at3[:, :, :], three(4), db3[:, :, :], ALU.mult).then_inc(at_ready, 1)
                st(v.tensor_tensor(qkd[:, :, :], three(5), dt3[:, :, :], ALU.mult))
                v.tensor_tensor(qn, qn, egb[:], ALU.mult).then_inc(qd_ready, 1)
                dve.wait_ge(lt_ready, len(LEVELS) * h + 1)
                v.tensor_tensor(tt[:, :, :], ident[:].unsqueeze(1).to_broadcast([P, UNITS, P]),
                                lt[:, 0, :].rearrange("p (u n) -> p u n", u=UNITS), ALU.subtract).then_inc(t_ready, 1)
                dve.wait_ge(turn_done, h1)
                v.tensor_copy(tn[:, :, :], three(4)).then_inc(t_ready, 1)
                dve.wait_ge(tok_read, 2 * h1)
                dve.wait_ge(ks_done, 2 * h + 1)
                v.scalar_tensor_tensor(vb[0:NS, 2, :], ps[7][0:NS, 384:512], hs[0:NS, NBEG + 2:NBEG + 3], vb[0:NS, 2, :],
                                       ALU.mult, ALU.add).then_inc(r_ready, 1)
                for l in range(1, len(LEVELS)):
                    units = UNITS if l < SAMPLE_LEVELS else 2
                    if l < len(LEVELS) - 1:
                        dve.wait_ge(dd_done, 11 * h + 2 * l - 1)
                        v.tensor_tensor(tn[:, 0:units, :], tn[:, 0:units, :], three(5)[:, 0:units, :], ALU.subtract)\
                            .then_inc(t_ready, 1)
                    dve.wait_ge(dd_done, 11 * h + min(2 * l, 11))
                    v.tensor_tensor(tt[:, 0:units, :], tt[:, 0:units, :], three(6)[:, 0:units, :], ALU.subtract).then_inc(t_ready, 1)
                dve.wait_ge(ks_done, 2 * h + 2)
                v.scalar_tensor_tensor(vb[:, 1, :], ps[7][:, 2 * P:3 * P], hs[:, NBEG + 1:NBEG + 2], vb[:, 1, :],
                                       ALU.mult, ALU.add).then_inc(r_ready, 1)
                dve.wait_ge(so_done, h1)
                dve.wait_ge(s2_out, 16 * h)
                v.scalar_tensor_tensor(s2, s1, hs[:, EGL + 1:EGL + 2], ps[4][:, P:2 * P], ALU.mult, ALU.add)\
                    .then_inc(state_ready, 1)
                dve.wait_ge(sc_done, h1)
                dve.wait_ge(sn_done, 2 * h1)
                st(v.tensor_tensor(sin[:, 0:4, :], sin[:, 0:4, :], ps[6][:, :].rearrange("p (b e) -> p b e", b=4), ALU.add))
                v.tensor_tensor(sin[:, 4:8, :], sin[:, 4:8, :], ps[7][:, :].rearrange("p (b e) -> p b e", b=4), ALU.add)\
                    .then_inc(sn_ready, 1)
                dve.wait_ge(oss_done, h1)
                v.tensor_scalar(rs[:], ps[4][:, 0:TOKENS], 1.0 / P, EPS, ALU.mult, ALU.add).then_inc(orm_ready, 1)
                dve.wait_ge(ort_ready, h1)
                st(v.reciprocal(rs[:], rs[:]))
                st.wait()
                st(v.tensor_tensor(rs[:], rs[:], ps[5][:, 0:TOKENS], ALU.mult))
                st.wait()
                v.scalar_tensor_tensor(oT[:, h, :], rs[:], half[:, CT:CT + 1], zs, ALU.mult, ALU.mult).then_inc(o_done, 1)
                st.leave(H)
            dve.wait_ge(ln_done, 1)
            st(v.tensor_scalar(mean[:], ps[4][:, 0:TOKENS], 1.0 / 1024, None, ALU.mult))
            st.wait()
            over = mean[:].unsqueeze(1).to_broadcast([P, CT, TOKENS])
            v.tensor_tensor(cT, cT, over, ALU.subtract).then_inc(ln_v, 1)
            st(v.memset(r3[:], 1.0))
            st(v.memset(seven[:, 0:2 * 576], 0.0))
            st.wait()
            for a in range(AH):
                done = FIRST["att"] + 6 * a
                dve.wait_ge(att_q, 2 * a + 2)
                for d in two:
                    last = v.tensor_copy(qm[:, d, :].rearrange("p (b s) -> p b s", s=72)[:, :, 0:TS],
                                         xq[:, d, TP:].rearrange("p (b s) -> p b s", b=NBATCH))
                last.then_inc(qm_ready, 1)
                if a == 0:
                    dve.wait_ge(ln_done, 2)
                    v.tensor_scalar(rs[:], ps[5][:, 0:TOKENS], 1.0 / 1024, EPS, ALU.mult, ALU.add).then_inc(ln_v, 1)
                    dve.wait_ge(ln_a, 2)
                    st(v.reciprocal(rs[:], rs[:]))
                    st.wait()
                    st(v.scalar_tensor_tensor(cT, cT, 0.5, rs[:].unsqueeze(1).to_broadcast([P, CT, TOKENS]), ALU.mult, ALU.mult))
                    st.wait()
                    for c in range(CT):
                        last = v.tensor_scalar(cT[:, c, :], cT[:, c, :], cst[:, C_LNG + c:C_LNG + c + 1], half[:, c:c + 1], ALU.mult, ALU.add)
                    last.then_inc(ln_v, 1)
                    dve.wait_ge(ln_a, 3)
                    v.scalar_tensor_tensor(cT, lnsq, 1.0, cT, ALU.add, ALU.mult).then_inc(ln_v, 1)
                dve.wait_ge(tiles_done, done + 4)
                st(v.tensor_reduce(mx[:, 0:2], ps[2].rearrange("p (t m) -> p t m", t=2), AX, ALU.max))
                st(v.tensor_reduce(mx[0:NS, 2:3], ps[3][0:NS, 0:MEM], AX, ALU.max))
                st.wait()
                v.tensor_scalar(mx[:, 0:2], mx[:, 0:2], -1.0 / 16.0, None, ALU.mult)
                v.tensor_scalar(mx[0:NS, 2:3], mx[0:NS, 2:3], -1.0 / 16.0, None, ALU.mult).then_inc(mx_ready, 1)
                dve.wait_ge(pexp_ready, a + 1)
                st(v.reciprocal(sm[:, 0:2], sm[:, 0:2]))
                st(v.reciprocal(sm[0:NS, 2:3], sm[0:NS, 2:3]))
                st.wait()
                for t in range(UNITS):
                    n = P if t < 2 else NS
                    last = v.tensor_scalar(pp[0:n, t, :], pp[0:n, t, :], sm[0:n, t:t + 1], None, ALU.mult)
                last.then_inc(pn_ready, 1)
                dve.wait_ge(pt_done, a + 1)
                v.tensor_copy(pT[:, :, TP:], ps[7][:, 0:P].rearrange("p (m t) -> p m t", m=2)).then_inc(pt_ready, 1)
                dve.wait_ge(tiles_done, done + 6)
                v.tensor_copy(xoT[:, 2 * a, :], ps[4][:, 0:TOKENS])
                v.tensor_copy(xoT[:, 2 * a + 1, :], ps[5][:, 0:TOKENS]).then_inc(ao_read, 1)
            dve.wait_ge(s2_out, 16 * H)
            with dve.Fori(0, KT) as i:
                st.enter(i, 1)
                dve.wait_ge(merged_ready, i)
                for n, (bank, tile) in enumerate(((1, 2), (3, 4), (5, 5))):
                    dve.wait_ge(gate_done, 3 * i + n + 1)
                    dve.wait_ge(tiles_done, FIRST["merge"] + 5 * i + tile)
                    v.scalar_tensor_tensor(t3[:, n, :], g3[:, n, :], 1.0, ps[bank][:, 0:TOKENS], ALU.add, ALU.mult).then_inc(merge_read[n], 1)
                    if n == 1:
                        dve.wait_ge(merge_read[1], i + 1)
                        st(v.tensor_tensor(t3[:, 0, :], t3[:, 0, :], t3[:, 1, :], ALU.add))
                dve.wait_ge(merge_read[2], i + 1)
                st.wait()
                v.tensor_tensor(mm[:, i, :], t3[:, 0, :], t3[:, 2, :], ALU.add).then_inc(merged_ready, 1)
                st.leave(KT)
            with dve.Fori(0, 4) as i:
                for j in range(4):
                    dve.wait_ge(tiles_done, FIRST["out"] + 4 * i + j + 1)
                    x = xT[:, 4 * i + j, :]
                    v.scalar_tensor_tensor(x, ps[6 + j % 2][:, 0:TOKENS], 0.5, x, ALU.mult, ALU.add).then_inc(out_read[j % 2], 1)
            finish_norm(3, xT, hT, C_FFN, TOKENS, 5, D)
            dve.wait_ge(r3_a, 3)
            dve.wait_ge(norm_ready, 3)
            dve.wait_ge(consts_ready, 2)
            st(v.memset(sc[NS:P, :, 2 * P:], 0.0))
            v.memset(wz[:, :, :, :], 0.0).then_inc(dotted[0], SLOTS)
            v.memset(efull[:, :, :], 0.0).then_inc(dotted[1], SLOTS)
            v.tensor_scalar(r3[:], r3[:], 1.0 / D, EPS, ALU.mult, ALU.add).then_inc(r3_v, 1)
            dve.wait_ge(r3_a, 4)
            v.reciprocal(r3[:], r3[:]).then_inc(r3_v, 1)
            st.wait()
            combos = [(x, t) for x in two for t in range(UNITS)]
            with dve.Fori(0, 4) as i:
                st.enter(i, TOPK_STEPS)
                for q in two:
                    head_at = (2 * i + q) * TOPK
                    dve.to_reg(2 * i + q + 1)
                    dve.wait_ge(r3_a, 4)
                    for x in two:
                        dve.wait_ge(scores_read[x], 2 * i + q + 1)

                    def lst(x, t):
                        return sc[:, 2 * q + x, t * P:(t + 1) * P]

                    def lst2(x, t):
                        return sc2[:, x, t * P:(t + 1) * P]

                    for x, t in combos:
                        st(v.max(v16[:, x, t, 0:8], lst(x, t)))
                    st.wait_after(r3_a, 4)
                    for x, t in combos:
                        st(v.max_index(iu[:, x, t, 0:8], v16[:, x, t, 0:8], lst(x, t)))
                    for x, t in combos:
                        st(v.match_replace(lst2(x, t), v16[:, x, t, 0:8], lst(x, t), NEG))
                    st.wait_after(r3_a, 4)
                    for x, t in combos:
                        st(v.max(v16[:, x, t, 8:16], lst2(x, t)))
                    st.wait_after(r3_a, 4)
                    for n, (x, t) in enumerate(combos):
                        st(v.max_index(iu[:, x, t, 8:16], v16[:, x, t, 8:16], lst2(x, t)))
                    st(v.tensor_tensor(cand[:, :, :].rearrange("p t (a b) -> p t a b", a=TOPK),
                                       v16[:, 0].unsqueeze(3).to_broadcast([P, UNITS, TOPK, TOPK]),
                                       v16[:, 1].unsqueeze(2).to_broadcast([P, UNITS, TOPK, TOPK]), ALU.add))
                    st.wait()
                    v.tensor_copy(i16, iu).then_inc(topk_read[q], 1)
                    for t in range(UNITS):
                        st(v.max(top[:, t, 0:8], cand[:, t, :]))
                    st.wait_after(r3_a, 4)
                    for t in range(UNITS):
                        st(v.max_index(pos[:, t, 0:8], top[:, t, 0:8], cand[:, t, :]))
                        st(v.match_replace(cand2[:, t, :], top[:, t, 0:8], cand[:, t, :], NEG))
                    st.wait_after(r3_a, 4)
                    for t in range(UNITS):
                        st(v.max(top[:, t, 8:16], cand2[:, t, :]))
                    st.wait_after(r3_a, 4)
                    for t in range(UNITS):
                        st(v.max_index(pos[:, t, 8:16], top[:, t, 8:16], cand2[:, t, :]))
                    v.tensor_tensor(gx[:, :, :], top[:, :, :], top[:, :, 0:1].to_broadcast([P, UNITS, TOPK]), ALU.subtract)\
                        .then_inc(soft_in, 1)
                    st.wait()
                    flat = pos[:, :, :].rearrange("p t k -> p (t k)")
                    st(v.tensor_scalar(digits[:, 0, :], flat, 4, None, ALU.logical_shift_right))
                    st(v.tensor_scalar(digits[:, 1, :], flat, 15, None, ALU.bitwise_and))
                    st.wait()
                    st(v.tensor_copy(fdig[:, :, :], digits[:, :, :]))
                    st.wait()
                    for x in two:
                        st(v.tensor_tensor(eq, fdig[:, x, :].unsqueeze(2).to_broadcast([P, UNITS * TOPK, TOPK]),
                                           iota16[:].unsqueeze(1).to_broadcast([P, UNITS * TOPK, TOPK]), ALU.is_equal))
                        st.wait()
                        e4 = eq.rearrange("p (t k) r -> p t k r", t=UNITS)
                        st(v.tensor_tensor(e4, e4, i16[:, x].unsqueeze(2).to_broadcast([P, UNITS, TOPK, TOPK]), ALU.mult))
                        st.wait()
                        st(v.tensor_reduce(e12[:, x, :], eq, AX, ALU.add))
                        st.wait()
                    st(v.scalar_tensor_tensor(efull[:, :, bass.ds(head_at, TOPK)], e12[:, 0, :].rearrange("p (t k) -> p t k", t=UNITS),
                                              float(NK), e12[:, 1, :].rearrange("p (t k) -> p t k", t=UNITS), ALU.mult, ALU.add))
                    dve.wait_ge(soft_out, 2 * i + q + 1)
                    st(v.tensor_reduce(gsum, gx[:, :, :], AX, ALU.add))
                    st.wait()
                    st(v.reciprocal(gsum, gsum))
                    st.wait()
                    v.tensor_tensor(gfull[:, :, bass.ds(head_at, TOPK)], gx[:, :, :],
                                    gsum.unsqueeze(2).to_broadcast([P, UNITS, TOPK]), ALU.mult).then_inc(picked, 1)
                    dve.wait_ge(picked, 2 * i + q + 1)
                st.leave(4)
            dve.wait_ge(lists_turned, 1)
            v.tensor_copy(eT, ps[0][:, 0:TOKENS]).then_inc(lists_ready, 1)
            v.tensor_copy(gT, ps[1][:, 0:TOKENS]).then_inc(lists_ready, 1)
            with dve.Fori(0, PAIRS) as i:
                for r in range(2 * group):
                    s, g_, j = r % 4, r // group, r % group
                    dve.wait_ge(u_in[s], 64 * i + 16 * (r // 4) + 16)
                    for half_ in two:
                        dve.wait_ge(spread, 32 * i + 2 * r + half_ + 1 + 2 * SLOTS)
                        u = ring[:, s, half_ * 1024:(half_ + 1) * 1024]
                        x = psum[:, 2 * half_:2 * half_ + 2, :].rearrange("p b n -> p (b n)")
                        v.tensor_tensor_reduce(out=u, in0=u, in1=x, scale=1.0, scalar=0.0, op0=ALU.mult, op1=ALU.add,
                                                     accum_out=dots[:, g_, j, half_:half_ + 1]).then_inc(dotted[half_], 1)
            for t in range(UNITS):
                n = P if t < 2 else NS
                y = ring[0:n, t, :]
                dve.wait_ge(parts_out, 96)
                v.tensor_tensor(y, y, x2tok[0:n, t, :], ALU.add).then_inc(r3_v, 1)
                dve.wait_ge(r3_a, 4 + 2 * t + 1)
                v.tensor_scalar(r3[0:n, t:t + 1], r3[0:n, t:t + 1], 1.0 / D, EPS, ALU.mult, ALU.add).then_inc(r3_v, 1)
                dve.wait_ge(r3_a, 4 + 2 * t + 2)
                st(v.reciprocal(r3[0:n, t:t + 1], r3[0:n, t:t + 1]))
                st.wait()
                dve.wait_ge(in_late, 48)
                v.scalar_tensor_tensor(y, y, r3[0:n, t:t + 1], grow[0:n, :], ALU.mult, ALU.mult).then_inc(r3_v, 1)

        @block.gpsimd
        def _(pool):
            g = nc.gpsimd
            st = Steps(pool, pool_step)

            def select(out, pattern, base, mult, op=ALU.is_ge, fill=0.0):
                st.wait()
                st(g.affine_select(out=out, in_=out, compare_op=op, fill=fill, base=base, pattern=pattern, channel_multiplier=mult))

            st(g.memset(ones[:], 1.0))
            st.wait()
            g.memset(sin, 0.0).then_inc(consts_ready, 1)
            st(g.memset(ident[:], 0.0))
            select(ident[:], [[-1, P]], 0, 1, ALU.not_equal, 1.0)
            st(g.memset(mu3[:, :, :], 1.0))
            st(g.memset(blk[:], 1.0))
            st(g.memset(bm[:], 1.0))
            st(g.memset(lm[:, :, :], 0.0))
            select(mu3[:, :, :], [[0, UNITS], [1, P]], 0, -1)
            nb = P // TS
            for m in (blk[:], mu3[:, 2, :]):
                grid = m.rearrange("p (n s) -> p n s", s=TS)
                select(grid, [[-TS, nb], [0, TS]], 0, 1)
                select(grid, [[TS, nb], [0, TS]], TS - 1, -1)
            select(bm[:], [[-TS, NBATCH]], 0, 1)
            select(bm[:], [[TS, NBATCH]], TS - 1, -1)
            for l, s in enumerate(LEVELS):
                low = lm[:, l, :].rearrange("p (n two s) -> p n two s", two=2, s=s)[:, :, 1, :]
                n = P // (2 * s)
                st.wait()
                st(g.memset(low, 1.0))
                select(low, [[-2 * s, n], [0, s]], 0, 1)
                select(low, [[2 * s, n], [0, s]], s - 1, -1)
            st(g.iota(iota16[:], [[1, TOPK]], base=0, channel_multiplier=0, allow_small_or_imprecise_dtypes=True))
            st(g.memset(onesb[:], 1.0))
            st.wait()
            g.memset(um, 0.0).then_inc(consts_ready, 1)
            pool.wait_ge(sp_c, 2)
            with pool.Fori(0, H) as h:
                h1 = h + 1
                st.enter(h, 1)
                pool.wait_ge(sc_done, h)
                pool.wait_ge(sp_c, 2)
                st(g.tensor_copy(hs_pool[:], hp[:, h, :]))
                st.wait()
                pool.wait_ge(rows_done, h)
                for out_, at_ in ((gb, GRAW), (bb, BETA)):
                    last = g.tensor_tensor(out_[:, :, :], ones[:].unsqueeze(1).to_broadcast([P, UNITS, P]),
                                           hs_pool[:, at_:at_ + UNITS].unsqueeze(2).to_broadcast([P, UNITS, P]), ALU.mult)
                last.then_inc(gb_ready, 1)
                pool.wait_ge(at_ready, h1)
                for l in range(len(LEVELS)):
                    units = UNITS if l < SAMPLE_LEVELS else 2
                    g.tensor_tensor(lt[:, l, 0:units * P].rearrange("p (u n) -> p u n", u=units), at3[:, 0:units, :],
                                    lm[:, l, :].unsqueeze(1).to_broadcast([P, units, P]), ALU.mult).then_inc(lt_ready, 1)
                pool.wait_ge(u_ready, 2 * h + 1)
                g.tensor_tensor(um, uu[:, 1, :].unsqueeze(1).to_broadcast([P, NBATCH, P]),
                                bm[:].unsqueeze(2).to_broadcast([P, NBATCH, P]), ALU.mult).then_inc(um_ready, 1)
                pool.wait_ge(so_done, h1)
                g.tensor_tensor(sin, sin, hs_pool[:, EGLB:EGLB + NBATCH].unsqueeze(2).to_broadcast([P, NBATCH, P]),
                                ALU.mult).then_inc(sc_done, 1)
                st.leave(H)
            pool.wait_ge(r3_v, 2)
            pool.wait_ge(in_late, 32)
            for t in range(UNITS):
                n = P if t < 2 else NS
                x = h2[0:n, :]
                if t:
                    pool.wait_ge(parts_out, 16 * t)
                st(g.tensor_scalar(x, x2tok[0:n, t, :], r3[0:n, t:t + 1], None, ALU.mult))
                st.wait()
                st(g.tensor_tensor(x, x, grow[0:n, :], ALU.mult))
                for m in range(3):
                    st.wait()
                    part = g.tensor_copy(parts[0:n, m, :], x)
                    if m < 2:
                        st(part)
                    else:
                        part.then_inc(parts_ready, 1)
                    if m < 2:
                        st.wait()
                        st(g.tensor_tensor(x, x, parts[0:n, m, :], ALU.subtract))
            pool.wait_ge(lists_ready, 2)
            with pool.Fori(0, PAIRS) as i:
                for g_ in two:
                    g.tensor_copy(idx8[:, g_, :], eT[:, bass.ds(16 * i + 8 * g_, group)]).then_inc(idx_ready, 1)
                    pool.wait_ge(idx_ready, 2 * i + g_ + 1)
                    for j in range(group):
                        s, n = j % 4, 16 * i + group * g_ + j
                        at_ = bass.IndirectOffsetOnAxis(ap=idx8[:, g_, j:j + 1], axis=0)
                        pool.to_reg(n + 1)
                        pool.wait_ge(lists_ready, 2)
                        pool.wait_ge(dotted[1], n + 1)
                        g.indirect_dma_start(ring[:, s, :], None, io["peer_u"], at_).then_inc(u_in[s], 16)
                        pool.wait_ge(lists_ready, 2)
                        pool.wait_ge(summed, n + 1)
                        g.indirect_dma_start(ring[:, 4 + s, :], None, io["peer_v"], at_).then_inc(v_in[s], 16)



def tiles(w):
    k, n = w.shape
    return np.ascontiguousarray(w.reshape(k // P, P, n // P, P).transpose(2, 1, 0, 3).reshape(n // P, P, k))


def cols(v):
    return v.reshape(-1, P).T


_OUTS = {"y": (TOKENS, D), "mem_k": (P, CT, MEM), "mem_v": (P, 2, 1024), "conv_out": (CT, P, CWIN), "qkv_out": (H, P, 3, QWIN),
         "delta_p": (H, P, P), "delta_s": (NBATCH, H, P, P)}


def layouts(a):
    w_in = a["w_in"][0]
    pieces = np.split(w_in, np.cumsum([1024, 1024, 6144, 2048, 16, 16, 1024, D, D]), axis=1)
    glu_a, glu_g, qkv, z, w_a, w_b, xq, g_conv, g_dn, g_xa = pieces
    x = np.concatenate([a["x_prompt"][0], a["x_sample"].reshape(NS, D)], 0)
    arr = {}
    arr["xT"] = x.T.reshape(KT, P, TOKENS).transpose(1, 0, 2)
    arr["memT"] = a["mem_prompt"][0].T.reshape(KT, P, MEM).transpose(1, 0, 2)
    dw = a["conv_dw"][0].T.reshape(CT, P, CK).transpose(1, 0, 2).reshape(P, CT * CK)
    dnw = a["dn_conv_w"][0].T.reshape(3, H, P, QK).transpose(2, 1, 0, 3).reshape(P, H * 3 * QK)
    arr["consts"] = np.concatenate([cols(a["norm_mem"][0]), cols(a["norm_mix"][0]), cols(a["norm_ffn"][0]), cols(a["conv_ln_g"][0]),
                                    cols(a["conv_ln_b"][0]), cols(a["conv_dw_b"][0]), dw, dnw, cols(a["dn_norm_g"][0])], 1)
    arr["dn_rows"] = np.concatenate([a["dn_a_log"][0], a["dn_dt_bias"][0]])
    arr["w_ab"] = np.concatenate([w_a, w_b], 1).reshape(KT, P, 32).transpose(1, 0, 2).reshape(P, KT * 32)
    arr["w_mem"] = tiles(a["w_mem_kv"][0])
    arr["w_glu"] = np.stack([tiles(glu_a), tiles(glu_g)], 1).reshape(2 * CT, P, D)
    q, k, v = (tiles(t) for t in np.split(qkv, 3, axis=1))
    arr["w_head"] = np.stack([q, k, v, tiles(z)], 1).reshape(4 * H, P, D)

    def windows(state, n_new):
        b, k1, c = state.shape
        s = state.transpose(2, 0, 1).reshape(c // P, P, b, k1)
        return np.concatenate([s, np.zeros(s.shape[:3] + (n_new,), s.dtype)], 3)

    arr["conv_in"] = windows(a["state_conv"][0], TS).reshape(CT, P, NBATCH * CWIN_S)
    arr["qkv_in"] = windows(a["state_qkv_conv"][0], TS).reshape(3, H, P, NBATCH * QWIN_S).transpose(1, 2, 0, 3)
    arr["delta_in"] = a["state_delta"][0]
    kc = a["cache_mem_k"][0].reshape(2, 4, MEM, AH, 2, P).transpose(3, 0, 5, 1, 4, 2).reshape(AH, 2, P, D)
    vc = a["cache_mem_v"][0].reshape(2, 4, 2, P, AH, 256).transpose(4, 0, 3, 1, 2, 5).reshape(AH, 2, P, D)
    arr["w_att"] = np.concatenate([tiles(xq).reshape(AH, 2, P, D), kc, vc], 1).reshape(6 * AH, P, D)
    gates = [tiles(w) for w in (g_conv, g_dn, g_xa)]
    outer = np.concatenate([tiles(a["w_conv_out"][0]), tiles(a["w_xa_out"][0])], 2)
    arr["w_merge"] = np.stack([gates[0], outer, gates[1], tiles(a["w_dn_out"][0]), gates[2]], 1).reshape(5 * KT, P, D)
    arr["w_outp"] = tiles(a["w_out"][0])
    arr["w_pq"] = tiles(a["w_peer_q"][0])
    arr["keysT"] = np.stack([a["peer_keys_1"][0].T, a["peer_keys_2"][0].T], 1)
    arr["g_rows"] = np.stack([a["norm_ffn"][0], a["norm_final"]])
    arr["peer_u"] = a["peer_u"][0]
    arr["peer_v"] = a["peer_v"][0]
    return {k: np.ascontiguousarray(v) for k, v in arr.items()}


def results(o):
    y = o["y"]
    k = o["mem_k"].transpose(2, 1, 0).reshape(1, 1, MEM, AH, 256)
    v = o["mem_v"].transpose(1, 0, 2).reshape(1, 1, MEM, AH, 256)
    cw = o["conv_out"].reshape(1024, CWIN)
    conv_p = cw[:, TP:TP + CK - 1].T[None, None]
    conv_s = cw[:, CK - 1 + TP:].reshape(1024, NBATCH, CWIN_S)[:, :, TS:].transpose(1, 2, 0)[None]
    qw = o["qkv_out"].transpose(2, 0, 1, 3).reshape(3 * H * P, QWIN)
    qkv_p = qw[:, TP:TP + QK - 1].T[None, None]
    qkv_s = qw[:, QWIN0:].reshape(3 * H * P, NBATCH, QWIN_S)[:, :, TS:].transpose(1, 2, 0)[None]
    out = (y[:TP].reshape(1, TP, D), y[TP:].reshape(NBATCH, TS, D), k, v, conv_p, qkv_p,
           o["delta_p"].reshape(1, 1, H, P, P), conv_s, qkv_s, o["delta_s"].reshape(1, NBATCH, H, P, P))
    return tuple(np.ascontiguousarray(x) for x in out)


def kernel(**inputs):
    import concourse.bacc as bacc
    from concourse.bass_utils import run_bass_kernel_spmd

    nc = bacc.Bacc("TRN2", target_bir_lowering=False, num_devices=1)
    arrays = layouts({k: np.asarray(v) for k, v in inputs.items()})
    io = {k: nc.dram_tensor(f"in_{k}", v.shape, F32, kind="ExternalInput").ap() for k, v in arrays.items()}
    for k, shape in _OUTS.items():
        io[k] = nc.dram_tensor(f"out_{k}", shape, F32, kind="ExternalOutput").ap()
    build(nc, io)
    r = run_bass_kernel_spmd(nc, [{f"in_{k}": v for k, v in arrays.items()}], core_ids=[0])
    return results({k: r.results[0][f"out_{k}"] for k in _OUTS})
```

```python
from contextlib import ExitStack

import numpy as np
import concourse.bass as bass
from concourse import mybir

F32 = mybir.dt.float32
BF16 = mybir.dt.bfloat16
U32 = mybir.dt.uint32
I32 = mybir.dt.int32
ACT = mybir.ActivationFunctionType
ALU = mybir.AluOpType
AX = mybir.AxisListType.X

P = 128
D = 2048
KT = D // P
TP, NBATCH, TS = 256, 8, 8
NS = NBATCH * TS
TOKENS = TP + NS
MEM = 256
CT = 1024 // P
CK = 31
CWIN_S = CK - 1 + TS
CWIN = CK - 1 + TP + NBATCH * CWIN_S
H = 16
QK = 4
QWIN_S = QK - 1 + TS
QWIN0 = QK - 1 + TP
QWIN = QWIN0 + NBATCH * QWIN_S
AH = 4
PH = 8
NK = 128
TOPK = 16
EPS = 1e-6
NEG = -3.0e38
UNITS = 3
UT = UNITS * P

GC, BETA, NBEG, KDEC, EGL, EGLB, GRAW, NHP = 0, 3, 6, 9, 12, 14, 22, 25
C_MEM, C_MIX, C_FFN, C_LNG, C_LNB, C_DWB, C_DW = 0, 16, 32, 48, 56, 64, 72
C_DNW = C_DW + CT * CK
C_DNG = C_DNW + H * 3 * QK
C_ALL = C_DNG + 1

STREAM = [("kv", 4, 4), ("glu", 4, 4), ("head", H, 4), ("att", AH, 6), ("merge", KT, 5), ("out", 4, 4), ("pq", 4, 4)]
AHEAD = 4
ATT_SLOTS = [0, 1] + (AH - 1) * [2, 3, 0, 1, 4, 5] + [2, 3, 4, 5]


def stream_plan():
    first, before, n, per_slot = {}, {}, 0, [0] * 8
    for name, iters, tiles in STREAM:
        first[name], before[name] = n, list(per_slot)
        n += iters * tiles
        for s in range(tiles):
            per_slot[s] += iters
    return first, before


FIRST, BEFORE = stream_plan()
LEVELS = [1, 2, 4, 8, 16, 32, 64]
T_STEPS = 2 * len(LEVELS) - 1
HEAD_STEPS = 30
TOPK_STEPS = 116
TOP, LEVEL_P, LEVEL_D = 12, 2, 2
SAMPLE_LEVELS = 3


class Steps:

    def __init__(self, eng, sem):
        self.eng, self.sem, self.base, self.n, self.total = eng, sem, 0, 0, 0

    def __call__(self, ins):
        self.n += 1
        ins.then_inc(self.sem, 1)
        return self.n

    def wait(self, n=None):
        self.eng.wait_ge(self.sem, self.base + (self.n if n is None else n))

    def wait_after(self, sem, count):
        self.eng.to_reg(self.base + self.n)
        self.eng.wait_ge(sem, count)
        self.wait()

    def enter(self, i, per):
        self.start, self.per = self.n + self.base, per
        self.base, self.n = self.start + i * per, 0

    def leave(self, iters):
        assert self.n == self.per, ("steps per iteration", self.n)
        self.base, self.n = 0, self.start + iters * self.per


def build(nc, io):
    with ExitStack() as ctx:
        def sb(name, shape, dt=F32):
            return ctx.enter_context(nc.sbuf_tensor(name, shape, dt))

        def sem(name):
            return ctx.enter_context(nc.semaphore(name))

        def view(flat, at, *shape):
            n = int(np.prod(shape))
            v = flat[:, at[0]:at[0] + n]
            at[0] += n
            assert at[0] <= flat.shape[1], (at, flat.shape)
            return v if len(shape) == 1 else v.rearrange("p (a b) -> p a b", a=shape[0])

        ring = sb("ring", [P, 8, D])
        xT = sb("xT", [P, KT, TOKENS])
        hT = sb("hT", [P, KT, TOKENS])
        mm = sb("mm", [P, KT, TOKENS])
        kmem = sb("kmem", [P, CT, MEM])
        vmem = sb("vmem", [P, 2, 1024])
        branches = sb("branches", [P, (H + CT + CT) * TOKENS])
        oT = branches[:, 0:H * TOKENS].rearrange("p (h t) -> p h t", h=H)
        cT = branches[:, H * TOKENS:(H + CT) * TOKENS].rearrange("p (h t) -> p h t", h=CT)
        xoT = branches[:, (H + CT) * TOKENS:].rearrange("p (h t) -> p h t", h=CT)
        cst = sb("cst", [P, C_ALL])
        ones = sb("ones", [P, P])
        ident = sb("ident", [P, P])
        rs = sb("rs", [P, TOKENS])
        mean = sb("mean", [P, TOKENS])
        lm = sb("lm", [P, len(LEVELS), P])
        mu3 = sb("mu3", [P, UNITS, P])
        blk = sb("blk", [P, P])
        bm = sb("bm", [P, NBATCH])
        ab = sb("ab", [P, UNITS, 32])
        hp = sb("hp", [P, H, NHP])
        hs = sb("hs", [P, NHP])
        hs_pool = sb("hs_pool", [P, NHP])
        pw = sb("pw", [P, 3 * QK])
        egb = sb("egb", [P, UT])

        at = [0]
        vT = view(branches, at, CT, MEM)
        cwin = view(branches, at, 2, CWIN)
        sg = view(branches, at, 2, TOKENS)
        assert at[0] <= H * TOKENS
        low = ring[:, 4:6, :].rearrange("p a b -> p (a b)")
        at = [0]
        qwin, qn, kn, vv = view(low, at, 3, QWIN), view(low, at, UT), view(low, at, UT), view(low, at, UT)
        dt3, db3, gb, bb = (view(low, at, UNITS, P) for _ in range(4))
        at = [0]
        six = ring[:, 6, :]
        sin, um = view(six, at, NBATCH, P), view(six, at, NBATCH, P)
        at = [0]
        seven = ring[:, 7, :]
        knm, qkd, tt, tn = view(seven, at, NBATCH * 72), view(seven, at, UNITS, P), view(seven, at, UNITS, P), view(seven, at, UNITS, P)
        zs = view(seven, at, TOKENS)
        mmf = mm[:, :, :].rearrange("p a b -> p (a b)")
        at = [0]
        lt = view(mmf, at, len(LEVELS), UT)
        kd, vb, uu, at3, pm = (view(mmf, at, UNITS, P) for _ in range(5))
        s1, s2 = view(mmf, at, P), view(mmf, at, P)
        xof = branches[:, (H + CT) * TOKENS:]
        at = [0]
        cv, th, nrm = view(xof, at, 3, TOKENS), view(xof, at, 3, TOKENS), view(xof, at, 2, TOKENS)
        sqo = mean[:]

        psum = ctx.enter_context(nc.psum_tensor("psum", [P, 8, 512], F32))
        ps = [psum[:, i, :] for i in range(8)]

        def three(bank):
            return ps[bank][:, 0:UT].rearrange("p (a b) -> p a b", a=UNITS)

        in_mem, in_x, in_cst, in_rows, in_ab = sem("in_mem"), sem("in_x"), sem("in_cst"), sem("in_rows"), sem("in_ab")
        w_in = [sem(f"w_in{i}") for i in range(6)]
        tiles_done = sem("tiles_done")
        consts_ready = sem("consts_ready")
        pool_step, dve_step = sem("pool_step"), sem("dve_step")
        sq_ready, ss_done, ms_ready, rt_ready, norm_ready = (sem(n) for n in ("sq_ready", "ss_done", "ms_ready", "rt_ready", "norm_ready"))
        v_turned, v_placed, stored = sem("v_turned"), sem("v_placed"), sem("stored")
        ab_done, ab_ready, sp_a, sp_b, sp_c = (sem(n) for n in ("ab_done", "ab_ready", "sp_a", "sp_b", "sp_c"))

        ab_w = sb("ab_w", [P, KT * 32])
        rows = sb("rows", [P, 32])
        two = range(2)
        kv_free = [sem(f"kv_free{j}") for j in range(4)]
        conv_read, cwin_in, cwin_out = ([sem(f"{n}{j}") for j in two] for n in ("conv_read", "cwin_in", "cwin_out"))
        proj_read = [sem(f"proj_read{j}") for j in range(4)]
        o_done = sem("o_done")
        qst_in, qwin_out, sin_in, sin_out, s2_out, sn_ready, sc_done, qd_ready, silu_ready = (sem(n) for n in (
            "qst_in", "qwin_out", "sin_in", "sin_out", "s2_out", "sn_ready", "sc_done", "qd_ready", "silu_ready"))
        gate_ready, cwin_full = ([sem(f"{n}{j}") for j in two] for n in ("gate_ready", "cwin_full"))
        gz = sb("gz", [P, 48 + P])
        dwp2 = sb("dwp2", [P, 2, CK + 1])
        half = sb("half", [P, CT + 1])
        sp3 = sb("sp3", [P, 4, 48])
        ex = sb("ex", [P, 144 + P])
        sp_v, sp_s = sem("sp_v"), sem("sp_s")
        gb_ready, rows_done, rows_used, sq_qk, ssq_done, nrm_ready, nrt_ready, qk_ready = (sem(n) for n in (
            "gb_ready", "rows_done", "rows_used", "sq_qk", "ssq_done", "nrm_ready", "nrt_ready", "qk_ready"))
        g_done, tok_done, tok_read, at_ready, lt_ready, t_ready, turn_done, p_done, p_ready, dd_done = (sem(n) for n in (
            "g_done", "tok_done", "tok_read", "at_ready", "lt_ready", "t_ready", "turn_done", "p_done", "p_ready", "dd_done"))
        v_ready, tanh_ready, dtx_ready, knm_ready, ks_done, r_ready = (sem(n) for n in (
            "v_ready", "tanh_ready", "dtx_ready", "knm_ready", "ks_done", "r_ready"))
        u_done, u_ready, s_done, s1_ready, um_ready, sn_done, so_done, osq_ready, oss_done, orm_ready, ort_ready = (sem(n) for n in (
            "u_done", "u_ready", "s_done", "s1_ready", "um_ready", "sn_done", "so_done", "osq_ready", "oss_done", "orm_ready", "ort_ready"))
        dt_ready, z_ready, conv_ready, state_ready = sem("dt_ready"), sem("z_ready"), sem("conv_ready"), sem("state_ready")

        at = [0]
        xq, pp, pT = view(six, at, 2, TOKENS), view(six, at, UNITS, MEM), view(six, at, 2, TOKENS)
        qm = seven[:, 0:2 * 576].rearrange("p (t n) -> p t n", t=2)
        xqs = (xq, seven[:, 2 * 576:2 * 576 + 2 * TOKENS].rearrange("p (t n) -> p t n", t=2))
        mx, sm, r3 = sb("mx", [P, UNITS]), sb("sm", [P, UNITS]), sb("r3", [P, UNITS])
        g3 = seven[:, 0:3 * TOKENS].rearrange("p (n t) -> p n t", n=3)
        t3 = six[:, 0:3 * TOKENS].rearrange("p (n t) -> p n t", n=3)
        lnsq = mmf[:, 0:CT * TOKENS].rearrange("p (c t) -> p c t", c=CT)
        x2tok = branches[:, 0:UNITS * D].rearrange("p (t d) -> p t d", t=UNITS)
        grow = kmem[:, :, :].rearrange("p a b -> p (a b)")
        h2 = vmem[:, :, :].rearrange("p a b -> p (a b)")
        parts = mmf.bitcast(BF16)[:, 0:3 * D].rearrange("p (n d) -> p n d", n=3)
        keys = sb("keys", [P, 2, NK])
        qs = six[:, 0:2 * TOKENS].rearrange("p (n t) -> p n t", n=2)
        at = [0]
        sc, sc2 = view(low, at, 4, UT), view(low, at, 2, UT)
        cand = view(low, at, UNITS, TOPK * TOPK)
        at = [0]
        cand2 = view(seven, at, UNITS, TOPK * TOPK)
        eq = view(seven, at, UNITS * TOPK * TOPK // 2).bitcast(BF16).rearrange("p (n r) -> p n r", r=TOPK)
        xflat = xT[:, :, :].rearrange("p a b -> p (a b)")
        at = [0]

        def small(*shape, dt=F32):
            v = view(xflat, at, int(np.prod(shape)))
            if dt != F32:
                v = v.bitcast(dt)
            names = "abc"[:len(shape)]
            sizes = dict(zip(names, shape))
            return v if len(shape) == 1 else v.rearrange(f"p ({' '.join(names)}) -> p {' '.join(names)}", **sizes)

        def lists(dt=F32):
            v = small(2 * UNITS * TOPK, dt=dt)
            return v.rearrange("p (x t k) -> p x t k", x=2, t=UNITS)

        v16, iu = lists(), lists(U32)
        i16 = small(UNITS * TOPK).bitcast(BF16).rearrange("p (x t k) -> p x t k", x=2, t=UNITS)
        fdig = small(UNITS * TOPK).bitcast(BF16).rearrange("p (x n) -> p x n", x=2)
        pos, digits = small(UNITS, TOPK, dt=U32), small(2, UNITS * TOPK, dt=U32)
        e12 = small(2, UNITS * TOPK)
        top, gx, gsum = small(UNITS, TOPK), small(UNITS, TOPK), small(UNITS)
        efull, gfull = small(UNITS, P), small(UNITS, P)
        eT, gT = small(TOKENS, dt=U32), small(TOKENS)
        iota16 = sb("iota16", [P, TOPK], BF16)
        hb = hT[:, :, :].rearrange("p a b -> p (a b)").bitcast(BF16)[:, 0:4 * D].rearrange("p (s d) -> p s d", s=4)
        onesb = sb("onesb", [P, P], BF16)
        wz = sb("wz", [P, 2, 8, 8])
        idx8 = sb("idx8", [P, 2, 8], U32)
        g8, dots, ge = sb("g8", [P, 2, 8]), sb("dots", [P, 2, 8, 2]), sb("ge", [P, 2, 8])
        osb = mmf[:, 0:D]
        hparts = nc.dram_tensor("hparts", (UT, 3, D), BF16, kind="Internal").ap()
        experts = nc.dram_tensor("experts", (TOKENS, D), F32, kind="Internal").ap()

        ln_done, ln_v, ln_a = sem("ln_done"), sem("ln_v"), sem("ln_a")
        att_q, qm_ready, mx_ready, pexp_ready, pn_ready, pt_done, pt_ready, ao_read = (sem(n) for n in (
            "att_q", "qm_ready", "mx_ready", "pexp_ready", "pn_ready", "pt_done", "pt_ready", "ao_read"))
        gate_done, merged_ready, x2_squared = sem("gate_done"), sem("merged_ready"), sem("x2_squared")
        merge_read = [sem(f"merge_read{n}") for n in range(3)]
        out_read = [sem(f"out_read{n}") for n in two]
        turned, turned_read, r3_v, r3_a, in_late, rest_ready, parts_out = (sem(n) for n in (
            "turned", "turned_read", "r3_v", "r3_a", "in_late", "rest_ready", "parts_out"))
        q_read, scores_done, scores_read = ([sem(f"{n}{j}") for j in two] for n in ("q_read", "scores_done", "scores_read"))
        topk_read = [sem(f"topk_read{j}") for j in two]
        soft_in, soft_out, picked, lists_turned, lists_ready = (sem(n) for n in ("soft_in", "soft_out", "picked", "lists_turned", "lists_ready"))
        hb_in, hb_before = (qst_in, qwin_out, sin_in, sin_out), 16 * H
        u_in, v_in = ([sem(f"{n}{s}") for s in range(4)] for n in ("u_in", "v_in"))
        SLOTS = 4
        part_taken = sem("part_taken")
        summed = sem("summed")
        spread, w_ready, ge_ready, idx_ready, g8_ready = sem("spread"), sem("w_ready"), sem("ge_ready"), sem("idx_ready"), sem("g8_ready")
        dotted, acc_read, experts_out = ([sem(f"{n}{s}") for s in two] for n in ("dotted", "acc_read", "experts_out"))
        group = 8
        PAIRS = TOKENS // (2 * group)
        SPANS = [(0, P // 16 + 1), (P // 16 + 1, 2 * P // 16 + 1), (2 * P // 16 + 1, PAIRS)]
        fy = mmf[:, D:2 * D]

        def tile_sum(pe, src, n, bank, count, scaled=ones):
            for kt in range(count):
                last = nc.tensor.matmul(ps[bank][:, 0:n], scaled[:], src[:, kt, 0:n], start=kt == 0, stop=kt == count - 1)
            return last

        block = ctx.enter_context(nc.Block())

        @block.sync
        def _(sp):
            sp.dma_start(mm[:, :, 0:MEM], io["memT"]).then_inc(in_mem, 16)
            sp.dma_start(cst[:], io["consts"]).then_inc(in_cst, 16)

            def load(stage, src, base, i, j):
                n = FIRST[stage] + base + j
                if not isinstance(base, int) or n >= AHEAD:
                    sp.wait_ge(tiles_done, n - AHEAD + 1)
                sp.dma_start(ring[:, j, :], src[base + j]).then_inc(w_in[j], 16)

            for i in range(4):
                for j in range(4):
                    load("kv", io["w_mem"], 4 * i, i, j)
                    if i == 0 and j == 1:
                        sp.dma_start(xT[:, :, :], io["xT"]).then_inc(in_x, 16)
                        sp.dma_start(ab_w[:], io["w_ab"]).then_inc(in_ab, 16)
                        sp.dma_start(rows[:, 0:32], io["dn_rows"].partition_broadcast(P)).then_inc(in_rows, 16)
            with sp.Fori(0, 4) as i:
                for j in range(4):
                    load("glu", io["w_glu"], 4 * i, i, j)
                    if j % 2 == 0:
                        sp.wait_ge(cwin_out[j // 2], 16 * i)
                        sp.wait_ge(conv_read[j // 2], i)
                        sp.dma_start(cwin[:, j // 2, CK - 1 + TP:], io["conv_in"][2 * i + j // 2]).then_inc(cwin_in[j // 2], 16)
            def window_in(h):
                sp.wait_ge(qwin_out, 16 * h)
                sp.wait_ge(v_ready, h)
                sp.dma_start(qwin[:, :, QWIN0:], io["qkv_in"][h]).then_inc(qst_in, 16)

            def states_in_out(h, store=True):
                if store:
                    sp.wait_ge(state_ready, h)
                    sp.dma_start(io["delta_p"][h - 1], s2).then_inc(s2_out, 16)
                    sp.wait_ge(sn_ready, h)
                    sp.dma_start(io["delta_s"][:, h - 1].rearrange("b d e -> d b e"), sin).then_inc(sin_out, 16)
                    sp.wait_ge(sin_out, 16 * h)
                sp.dma_start(sin, io["delta_in"][:, h].rearrange("b d e -> d b e")).then_inc(sin_in, 16)

            def head_tiles(h, js):
                for j in js:
                    load("head", io["w_head"], 4 * h, h, j)

            window_in(0)
            states_in_out(0, store=False)
            head_tiles(0, range(4))
            head_tiles(1, range(4))
            with sp.Fori(2, H) as h:
                window_in(h - 1)
                head_tiles(h, range(4))
                states_in_out(h - 1)
            def att_tiles(start, end):
                for k in range(start, end):
                    j = ATT_SLOTS[k]
                    if k == ATT_SLOTS.index(4):
                        sp.wait_ge(o_done, H)
                        sp.wait_ge(qwin_out, 16 * H)
                    sp.wait_ge(tiles_done, FIRST["att"] + k - AHEAD + 1)
                    sp.dma_start(ring[:, j, :], io["w_att"][k]).then_inc(w_in[j], 16)

            window_in(H - 1)
            states_in_out(H - 1)
            att_tiles(0, 4)
            sp.wait_ge(state_ready, H)
            sp.dma_start(io["delta_p"][H - 1], s2).then_inc(s2_out, 16)
            sp.wait_ge(sn_ready, H)
            sp.dma_start(io["delta_s"][:, H - 1].rearrange("b d e -> d b e"), sin).then_inc(sin_out, 16)
            att_tiles(4, len(ATT_SLOTS))
            with sp.Fori(0, KT) as i:
                for j in range(5):
                    load("merge", io["w_merge"], 5 * i, i, j)
            with sp.Fori(0, 4) as i:
                for j in range(4):
                    load("out", io["w_outp"], 4 * i, i, j)
            sp.wait_ge(out_read[0], 8)
            sp.dma_start(keys[:, :, :], io["keysT"]).then_inc(in_late, 16)
            sp.dma_start(grow, io["g_rows"][0].partition_broadcast(P)).then_inc(in_late, 16)
            with sp.Fori(0, 4) as i:
                for j in range(4):
                    load("pq", io["w_pq"], 4 * i, i, j)
            sp.wait_ge(parts_out, 48)
            sp.dma_start(grow, io["g_rows"][1].partition_broadcast(P)).then_inc(in_late, 16)
            sp.wait_ge(tiles_done, FIRST["pq"] + 16)
            for t, (start, end) in enumerate(SPANS):
                n = P if t < 2 else NS
                with sp.Fori(start, end) as i:
                    for r in range(2 * group):
                        s = r % 4
                        sp.wait_ge(spread, 32 * i + 2 * r + 2)
                        sp.dma_start(hb[0:3, s, :], hparts[16 * i + r]).then_inc(hb_in[s], 16)
                for g_ in two:
                    sp.wait_ge(experts_out[g_], 16 * min(8 * (t + 1), PAIRS))
                sp.wait_ge(in_late, 48 + 16 * t)
                sp.dma_start(fy[0:n, :], experts[t * P:t * P + n]).then_inc(parts_out, 16)
            sp.wait_ge(in_late, 96)
            sp.wait_ge(stored, 32)
            for s in cwin_out:
                sp.wait_ge(s, 16 * CT // 2)
            sp.wait_ge(qwin_out, 16 * H)
            sp.wait_ge(s2_out, 16 * H)
            sp.wait_ge(sin_out, 16 * H)

        @block.tensor
        def _(pe):
            mat = nc.tensor.matmul

            def arrived(stage, j, i):
                pe.wait_ge(w_in[j], 16 * (BEFORE[stage][j] + 1) + 16 * i)

            def project(bank, j, src, n, kts=KT, k0=0, free=(), close=True):
                for s, count in free:
                    pe.wait_ge(s, count)
                for kt in range(kts):
                    last = mat(ps[bank][:, 0:n], ring[:, j, (k0 + kt) * P:(k0 + kt + 1) * P], src[:, kt, 0:n],
                               start=kt == 0, stop=kt == kts - 1)
                if close:
                    last.then_inc(tiles_done, 1)

            pe.wait_ge(consts_ready, 1)
            for n, (bank, cols) in enumerate(((6, MEM), (7, TOKENS))):
                pe.wait_ge(sq_ready, n + 1)
                tile_sum(pe, hT, cols, bank, KT).then_inc(ss_done, 1)
            pe.wait_ge(norm_ready, 1)
            with pe.Fori(0, 4) as i:
                for j in range(4):
                    arrived("kv", j, i)
                    project(j, j, mm, MEM, free=((kv_free[j], i),))
            for g in range(4):
                pe.wait_ge(kv_free[2 * (g % 2)], 4)
                pe.wait_ge(kv_free[2 * (g % 2) + 1], 4)
                pe.wait_ge(consts_ready, 2)
                if g >= 2:
                    pe.wait_ge(v_placed, g - 1)
                for q in range(4):
                    c, m = 2 * g + q // 2, q % 2
                    last = nc.tensor.transpose(ps[g % 2][:, q * P:(q + 1) * P], vT[:, c, m * P:(m + 1) * P], ident[:])
                last.then_inc(v_turned, 1)
            pe.wait_ge(norm_ready, 2)
            with pe.Fori(0, 4) as i:
                for j in range(4):
                    arrived("glu", j, i)
                    project(4 + j, j, hT, TOKENS, free=((cwin_full[j // 2], i),))
            pe.wait_ge(in_ab, 16)
            pe.wait_ge(v_placed, 4)
            for t in range(UNITS):
                n = P if t < 2 else NS
                for kt in range(KT):
                    last = mat(ps[2][0:n, 32 * t:32 * t + 32], hT[:, kt, t * P:t * P + n], ab_w[:, 32 * kt:32 * kt + 32],
                               start=kt == 0, stop=kt == KT - 1)
            last.then_inc(ab_done, 1)
            def head(h, nxt):
                stage, tiles_, at_i = ("head", 4, nxt) if nxt is not None else ("att", 2, 0)
                pieces = [(j, kt) for j in range(tiles_) for kt in range(KT)]

                def fill(n):
                    for _ in range(min(n, len(pieces))):
                        j, kt = pieces.pop(0)
                        if kt == 0:
                            arrived(stage, j, at_i)
                            if j == 0:
                                pe.wait_ge(nrm_ready, H if nxt is None else nxt)
                            pe.wait_ge(proj_read[j], H if nxt is None else nxt)
                        last = mat(ps[j][:, 0:TOKENS], ring[:, j, kt * P:(kt + 1) * P], hT[:, kt, :],
                                   start=kt == 0, stop=kt == KT - 1)
                        if kt == KT - 1:
                            last.then_inc(tiles_done, 1)

                def squares():
                    pe.wait_ge(sq_qk, nxt + 1)
                    for n in two:
                        last = mat(ps[n][:, 0:TOKENS], ones[:], nrm[:, n, :], start=True, stop=True)
                    last.then_inc(ssq_done, 1)

                if h is None:
                    pe.wait_ge(kv_free[3], 4)
                    pe.wait_ge(v_placed, 4)
                    pe.wait_ge(sp_a, 1)
                    fill(32)
                    pe.wait_ge(ab_ready, 1)
                    mat(ps[4][:, 0:32], mu3[:, 0, :], gz[:, 0:32], start=True, stop=True)
                    mat(ps[4][:, 32:48], mu3[:, 2, :], gz[:, 32:48], start=True, stop=True)
                    mat(ps[4][:, 48:80], ones[:], gz[:, 0:32], start=True, stop=True)
                    mat(ps[4][:, 80:96], blk[:], gz[:, 32:48], start=True, stop=True)
                    mat(ps[4][:, 96:96 + P], ones[:], gz[:, 48:48 + P], start=True, stop=True).then_inc(sp_b, 1)
                    fill(64)
                    squares()
                    return
                h1 = h + 1
                fill(TOP)
                pe.wait_ge(gb_ready, h1)
                pe.wait_ge(sn_ready, h)
                for u in range(UNITS):
                    mat(ps[7][:, u * P:(u + 1) * P], gb[:, u, :], mu3[:, u, :], start=True, stop=True)
                for u in range(UNITS):
                    last = mat(ps[6][:, u * P:(u + 1) * P], bb[:, u, :], ident[:], start=True, stop=True)
                last.then_inc(rows_done, 1)
                fill(5)
                pe.wait_ge(qk_ready, h1)
                pe.wait_ge(o_done, h)
                for n, src in enumerate((kn, qn)):
                    for u in range(UNITS):
                        c = slice(u * P, (u + 1) * P)
                        last = mat(ps[4 + n][:, c], kn[:, c], src[:, c], start=True, stop=True)
                last.then_inc(g_done, 1)
                pe.wait_ge(rows_used, 2 * h1)
                pe.wait_ge(v_ready, h1)
                for bank, src in ((6, kn), (7, vv)):
                    for u in range(UNITS):
                        last = nc.tensor.transpose(ps[bank][:, u * P:(u + 1) * P], src[:, u * P:(u + 1) * P], ident[:])
                last.then_inc(tok_done, 1)
                fill(4)
                pe.wait_ge(knm_ready, h1)
                pe.wait_ge(sin_in, 16 * h1)
                pe.wait_ge(tok_read, 2 * h1)
                for b in range(NBATCH):
                    last = mat(ps[7][0:NS, 384:512], knm[:, b * NS:(b + 1) * NS], sin[:, b, :], start=b == 0, stop=b == NBATCH - 1)
                last.then_inc(ks_done, 1)
                fill(3)
                pe.wait_ge(t_ready, T_STEPS * h + 1)
                for u in range(UNITS):
                    last = nc.tensor.transpose(ps[4][:, u * P:(u + 1) * P], tt[:, u, :], ident[:])
                last.then_inc(turn_done, 1)
                fill(3)
                for l in range(1, len(LEVELS)):
                    units = UNITS if l < SAMPLE_LEVELS else 2
                    pe.wait_ge(t_ready, T_STEPS * h + 2 * l)
                    pe.wait_ge(lt_ready, len(LEVELS) * h + l + 1)
                    for u in range(units):
                        last = mat(ps[4][:, u * P:(u + 1) * P], lt[:, l, u * P:(u + 1) * P], tn[:, u, :], start=True, stop=True)
                    last.then_inc(p_done, 1)
                    fill(LEVEL_P)
                    pe.wait_ge(p_ready, 6 * h + l)
                    if l < len(LEVELS) - 1:
                        for u in range(units):
                            last = mat(ps[5][:, u * P:(u + 1) * P], tt[:, u, :], pm[:, u, :], start=True, stop=True)
                        last.then_inc(dd_done, 1)
                    for u in range(units):
                        last = mat(ps[6][:, u * P:(u + 1) * P], pm[:, u, :], tt[:, u, :], start=True, stop=True)
                    last.then_inc(dd_done, 1)
                    fill(LEVEL_D)
                pe.wait_ge(t_ready, T_STEPS * h + T_STEPS)
                pe.wait_ge(r_ready, 2 * h + 1)
                mat(ps[7][:, 0:P], tt[:, 0, :], vb[:, 0, :], start=True, stop=True)
                mat(ps[7][:, P:2 * P], tt[:, 2, :], vb[:, 2, :], start=True, stop=True).then_inc(u_done, 1)
                fill(3)
                if nxt is not None:
                    squares()
                pe.wait_ge(u_ready, 2 * h + 1)
                mat(ps[4][:, 0:P], kd[:, 0, :], uu[:, 0, :], start=True, stop=True).then_inc(s_done, 1)
                mat(ps[5][:, 0:P], uu[:, 0, :], qkd[:, 0, :], start=True, stop=True)
                pe.wait_ge(qd_ready, h1)
                mat(ps[5][:, 256:TOKENS], uu[:, 1, :], qkd[:, 2, 0:NS], start=True, stop=False, skip_group_check=True)
                for b in range(NBATCH):
                    c = slice(TP + b * TS, TP + (b + 1) * TS)
                    mat(ps[5][:, c], sin[:, b, :], qn[:, c], start=False, stop=b == NBATCH - 1, skip_group_check=True)
                pe.wait_ge(s1_ready, h1)
                mat(ps[7][:, 2 * P:3 * P], kn[:, P:2 * P], s1, start=True, stop=True).then_inc(ks_done, 1)
                pe.wait_ge(um_ready, h1)
                umf = um.rearrange("p b e -> p (b e)")
                mat(ps[6][:, :], kd[:, 2, :], umf[:, 0:512], start=True, stop=True).then_inc(sn_done, 1)
                pe.wait_ge(r_ready, 2 * h + 2)
                mat(ps[7][:, 0:P], tt[:, 1, :], vb[:, 1, :], start=True, stop=True).then_inc(u_done, 1)
                fill(3)
                pe.wait_ge(u_ready, 2 * h + 2)
                mat(ps[5][:, P:2 * P], uu[:, 2, :], qkd[:, 1, :], start=True, stop=False)
                mat(ps[5][:, P:2 * P], s1, qn[:, P:2 * P], start=False, stop=True)
                mat(ps[4][:, P:2 * P], kd[:, 1, :], uu[:, 2, :], start=True, stop=True).then_inc(so_done, 1)
                mat(ps[7][:, :], kd[:, 2, :], umf[:, 512:1024], start=True, stop=True).then_inc(sn_done, 1)
                fill(3)
                pe.wait_ge(osq_ready, h1)
                pe.wait_ge(state_ready, h1)
                mat(ps[4][:, 0:TOKENS], ones[:], sqo, start=True, stop=True).then_inc(oss_done, 1)
                fill(64)

            head(None, 0)
            with pe.Fori(0, H - 1) as h:
                head(h, h + 1)
            head(H - 1, None)
            pe.wait_ge(o_done, H)
            for q in two:
                pe.wait_ge(conv_read[q], 4)
            tile_sum(pe, cT, TOKENS, 4, CT).then_inc(ln_done, 1)
            def queries(a):
                for j in range(2):
                    arrived("att", j, a)
                    project(j, j, hT, TOKENS, free=((att_q, 2 * a),) if a else ())

            pe.wait_ge(ln_a, 1)
            tile_sum(pe, lnsq, TOKENS, 5, CT).then_inc(ln_done, 1)
            for a in range(AH):
                xq = xqs[a % 2]
                pe.wait_ge(att_q, 2 * a + 2)
                pe.wait_ge(qm_ready, a + 1)
                for t in two:
                    for d in two:
                        mat(ps[2][:, t * MEM:(t + 1) * MEM], xq[:, d, t * P:(t + 1) * P], kmem[:, 2 * a + d, :], start=d == 0, stop=d == 1)
                arrived("att", 2, a)
                arrived("att", 3, a)
                for b in range(NBATCH):
                    for d in two:
                        at_ = (b % 4) * 512 + d * MEM
                        last = mat(ps[3][0:NS, 0:MEM], qm[:, d, b * NS:(b + 1) * NS], ring[:, 2 + b // 4, at_:at_ + MEM],
                                   start=b + d == 0, stop=b == NBATCH - 1 and d == 1)
                    if b % 4 == 3:
                        last.then_inc(tiles_done, 1)
                if a + 1 < AH:
                    queries(a + 1)
                pe.wait_ge(pn_ready, a + 1)
                for m in two:
                    for t in two:
                        nc.tensor.transpose(ps[6][:, m * MEM + t * P:m * MEM + (t + 1) * P], pp[:, t, m * P:(m + 1) * P], ident[:])
                    last = nc.tensor.transpose(ps[7][:, m * NS:(m + 1) * NS], pp[0:NS, 2, m * P:(m + 1) * P], ident[0:NS, 0:NS])
                last.then_inc(pt_done, 1)
                pe.wait_ge(pt_ready, 2 * a + 2)
                pe.wait_ge(ln_v, 2)
                arrived("att", 4, a)
                arrived("att", 5, a)
                if a:
                    pe.wait_ge(ao_read, a)
                for d in two:
                    at_ = a * 256 + d * P
                    for m in two:
                        mat(ps[4 + d][:, 0:TP], vmem[:, m, at_:at_ + P], pT[:, m, 0:TP], start=m == 0, stop=m == 1)
                for b in range(NBATCH):
                    c = slice(TP + b * TS, TP + (b + 1) * TS)
                    for d in two:
                        for m in two:
                            at_ = (b % 4) * 512 + m * 256 + d * P
                            last = mat(ps[4 + d][:, c], ring[:, 4 + b // 4, at_:at_ + P], pT[:, m, c], start=m == 0, stop=m == 1)
                    if b % 4 == 3:
                        last.then_inc(tiles_done, 1)
            pe.wait_ge(ln_v, 4)
            pe.wait_ge(ao_read, AH)
            with pe.Fori(0, KT) as i:
                arrived("merge", 0, i)
                project(0, 0, hT, TOKENS, free=((merge_read[0], i),))
                arrived("merge", 1, i)
                project(1, 1, cT, TOKENS, kts=CT, close=False)
                project(5, 1, xoT, TOKENS, kts=CT, k0=CT, free=((merge_read[2], i),))
                arrived("merge", 2, i)
                project(2, 2, hT, TOKENS, free=((merge_read[1], i),))
                arrived("merge", 3, i)
                project(3, 3, oT, TOKENS)
                arrived("merge", 4, i)
                project(4, 4, hT, TOKENS)
            pe.wait_ge(merged_ready, KT)
            with pe.Fori(0, 4) as i:
                for j in range(4):
                    arrived("out", j, i)
                    project(6 + j % 2, j, mm, TOKENS, free=((out_read[j % 2], 2 * i + j // 2),))
            pe.wait_ge(x2_squared, KT)
            tile_sum(pe, hT, TOKENS, 5, KT).then_inc(ss_done, 1)
            for t in range(UNITS):
                n = P if t < 2 else NS
                for q in range(4):
                    if 4 * t + q >= 4:
                        pe.wait_ge(turned_read, 4 * t + q - 3)
                    for kt in range(4):
                        last = nc.tensor.transpose(ps[q][0:n, kt * P:(kt + 1) * P], xT[:, 4 * q + kt, t * P:t * P + n], ident[:])
                    last.then_inc(turned, 1)
            pe.wait_ge(norm_ready, 3)
            pe.wait_ge(in_late, 32)
            with pe.Fori(0, 4) as i:
                for j in range(4):
                    b, n = j % 2, 2 * i + j // 2
                    arrived("pq", j, i)
                    project(4 + b, j, hT, TOKENS, free=((q_read[b], n),))
                    pe.wait_ge(q_read[b], n + 1)
                    pe.wait_ge(scores_read[b], n)
                    for t in range(UNITS):
                        w = P if t < 2 else NS
                        last = mat(ps[6 + b][0:w, t * P:(t + 1) * P], qs[:, b, t * P:t * P + w], keys[:, j % 2, :], start=True, stop=True)
                    last.then_inc(scores_done[b], 1)
            pe.wait_ge(picked, PH)
            for n, src in enumerate((efull, gfull)):
                for t in range(UNITS):
                    w = P if t < 2 else NS
                    last = nc.tensor.transpose(ps[n][:, t * P:t * P + w], src[0:w, t, :], ident[0:w, 0:w])
                    if n == 0 and t < 2:
                        last.then_inc(*((spread, 2 * SLOTS) if t else (summed, SLOTS)))
            last.then_inc(lists_turned, 1)
            def spread_token(i, r):
                s = r % 4
                pe.wait_ge(hb_in[s], 64 * i + 16 * (r // 4) + 16 + hb_before)
                for half_ in two:
                    pe.wait_ge(dotted[half_], 16 * i + r + SLOTS)
                    for q in (2 * half_, 2 * half_ + 1):
                        last = mat(ps[q][:, :], onesb[0:3, :], hb[0:3, s, q * 512:(q + 1) * 512], start=True, stop=True)
                    last.then_inc(spread, 1)

            def pair(i, final=False):
                for r in range(2 * group):
                    s, g_ = r % 4, r // group
                    if r < 2 * group - 1:
                        spread_token(i, r + 1)
                    elif not final:
                        spread_token(i + 1, 0)
                    pe.wait_ge(w_ready, 16 * i + r + 1)
                    pe.wait_ge(v_in[s], 64 * i + 16 * (r // 4) + 16)
                    if r % group == 0:
                        pe.wait_ge(acc_read[g_], i)
                    for q in range(4):
                        last = mat(psum[32 * g_:32 * g_ + group, 4 + q, :], wz[:, g_, r % group, :], ring[:, 4 + s, q * 512:(q + 1) * 512],
                                   start=r % group == 0, stop=r % group == group - 1, skip_group_check=True)
                    last.then_inc(summed, 1)

            pe.wait_ge(lists_ready, 2)
            spread_token(0, 0)
            with pe.Fori(0, PAIRS - 1) as i:
                pair(i)
            pair(PAIRS - 1, final=True)

        @block.scalar
        def _(act):
            fn = nc.scalar.activation

            def rooted(n, cols, buf=None):
                act.wait_ge(ms_ready, n)
                fn(rs[:, 0:cols], rs[:, 0:cols], ACT.Sqrt).then_inc(rt_ready, 1)

            act.wait_ge(in_mem, 16)
            fn(hT[:, :, 0:MEM], mm[:, :, 0:MEM], ACT.Square).then_inc(sq_ready, 1)
            rooted(1, MEM)
            act.wait_ge(in_x, 16)
            act.wait_ge(ss_done, 1)
            fn(hT[:, :, :], xT[:, :, :], ACT.Square).then_inc(sq_ready, 1)
            rooted(2, TOKENS)
            with act.Fori(0, 2) as i:
                for j in range(4):
                    act.wait_ge(tiles_done, 4 * i + j + 1)
                    fn(kmem[:, 4 * i + j, :], ps[j][:, 0:MEM], ACT.Copy).then_inc(kv_free[j], 1)
            with act.Fori(0, 2) as i:
                for j in range(4):
                    act.wait_ge(tiles_done, 4 * i + j + 9)
                    fn(vT[:, 4 * i + j, :], ps[j][:, 0:MEM], ACT.Copy).then_inc(kv_free[j], 1)
            for j in range(4):
                act.wait_ge(kv_free[j], 4)
            act.dma_start(io["mem_k"], kmem[:, :, :]).then_inc(stored, 16)
            act.wait_ge(v_placed, 4)
            act.dma_start(io["mem_v"], vmem[:, :, :]).then_inc(stored, 16)
            with act.Fori(0, 4) as i:
                for q in range(2):
                    act.wait_ge(tiles_done, FIRST["glu"] + 4 * i + 2 * q + 2)
                    act.wait_ge(conv_read[q], i)
                    fn(sg[:, q, :], ps[5 + 2 * q][:, 0:TOKENS], ACT.Tanh, scale=0.5).then_inc(gate_ready[q], 1)
                    act.wait_ge(cwin_full[q], i + 1)
                    act.dma_start(io["conv_out"][2 * i + q], cwin[:, q, :]).then_inc(cwin_out[q], 16)
            act.wait_ge(ab_done, 1)
            for u in range(UNITS):
                n = P if u < 2 else NS
                last = fn(ab[0:n, u, :], ps[2][0:n, 32 * u:32 * u + 32], ACT.Copy)
            last.then_inc(sp_a, 1)
            act.wait_ge(sp_v, 1)
            fn(sp3[:, 1, :], sp3[:, 0, :], ACT.Exp, scale=-1.0).then_inc(sp_s, 1)
            fn(rows[:, 0:16], rows[:, 0:16], ACT.Exp).then_inc(sp_s, 1)
            act.wait_ge(sp_v, 2)
            fn(sp3[:, 1, :], sp3[:, 1, :], ACT.Ln).then_inc(sp_s, 1)
            fn(sp3[:, 3, :], sp3[:, 3, :], ACT.Tanh, scale=0.5).then_inc(sp_s, 1)
            act.wait_ge(sp_v, 3)
            fn(ex[:], ex[:], ACT.Exp).then_inc(sp_s, 1)

            act.wait_ge(sp_c, 2)
            def window(h, j):
                if j == 0:
                    act.wait_ge(qst_in, 16 * (h + 1))
                act.wait_ge(tiles_done, FIRST["head"] + 4 * h + j + 1)
                fn(qwin[:, j, QK - 1:QWIN0], ps[j][:, 0:TP], ACT.Copy)
                fn(qwin[:, j, QWIN0:].rearrange("p (b s) -> p b s", b=NBATCH)[:, :, QK - 1:],
                   ps[j][:, TP:TOKENS].rearrange("p (b s) -> p b s", b=NBATCH), ACT.Copy).then_inc(proj_read[j], 1)

            def store_window(h):
                for j in range(3):
                    act.wait_ge(proj_read[j], h + 1)
                act.dma_start(io["qkv_out"][h], qwin[:, :, :]).then_inc(qwin_out, 16)

            def tanh(h, j):
                act.wait_ge(conv_ready, 3 * h + j + 1)
                fn(th[:, j, :], cv[:, j, :], ACT.Tanh).then_inc(tanh_ready, 1)

            def squares(h):
                act.wait_ge(silu_ready, 2 * h + 2)
                fn(nrm[:, :, :], cv[:, 0:2, :], ACT.Square).then_inc(sq_qk, 1)

            def root(h):
                act.wait_ge(nrm_ready, h + 1)
                fn(nrm[:, :, :], nrm[:, :, :], ACT.Sqrt).then_inc(nrt_ready, 1)

            def head(h, nxt):
                h1 = h + 1
                act.wait_ge(tiles_done, FIRST["head"] + 4 * h + 4)
                act.wait_ge(o_done, h)
                fn(zs, ps[3][:, 0:TOKENS], ACT.Tanh, scale=0.5).then_inc(z_ready, 1)
                act.wait_ge(dt_ready, h1)
                fn(egb[:], ps[7][:, 0:UT], ACT.Exp).then_inc(rows_used, 1)
                fn(dt3[:, :, :], dt3[:, :, :], ACT.Exp).then_inc(dtx_ready, 1)
                act.wait_ge(tok_done, h1)
                for u in range(UNITS):
                    last = fn(kd[:, u, :], ps[6][:, u * P:(u + 1) * P], ACT.Copy, scale=hs[:, KDEC + u:KDEC + u + 1])
                last.then_inc(tok_read, 1)
                for u in range(UNITS):
                    last = fn(vb[:, u, :], ps[7][:, u * P:(u + 1) * P], ACT.Copy, scale=hs[:, BETA + u:BETA + u + 1])
                last.then_inc(tok_read, 1)
                if nxt is not None:
                    window(nxt, 0)
                for l in range(1, len(LEVELS)):
                    units = UNITS if l < SAMPLE_LEVELS else 2
                    act.wait_ge(p_done, 6 * h + l)
                    fn(pm[:, 0:units, :], three(4)[:, 0:units, :], ACT.Copy).then_inc(p_ready, 1)
                    if nxt is not None:
                        if l == 2:
                            window(nxt, 1)
                        if l == 3:
                            tanh(nxt, 0)
                        if l == 5:
                            tanh(nxt, 1)
                        if l == 6:
                            squares(nxt)
                act.wait_ge(u_done, 2 * h + 1)
                fn(uu[:, 0:2, :], three(7)[:, 0:2, :], ACT.Copy).then_inc(u_ready, 1)
                if nxt is not None:
                    window(nxt, 2)
                    store_window(nxt)
                act.wait_ge(s_done, h1)
                act.wait_ge(s2_out, 16 * h)
                fn(s1, ps[4][:, 0:P], ACT.Copy).then_inc(s1_ready, 1)
                if nxt is not None:
                    tanh(nxt, 2)
                act.wait_ge(u_done, 2 * h + 2)
                fn(uu[:, 2, :], ps[7][:, 0:P], ACT.Copy).then_inc(u_ready, 1)
                if nxt is not None:
                    root(nxt)
                act.wait_ge(so_done, h1)
                fn(sqo, ps[5][:, 0:TOKENS], ACT.Square).then_inc(osq_ready, 1)
                act.wait_ge(orm_ready, h1)
                fn(rs[:], rs[:], ACT.Sqrt).then_inc(ort_ready, 1)

            for j in range(3):
                window(0, j)
            store_window(0)
            for j in range(3):
                tanh(0, j)
            squares(0)
            root(0)
            with act.Fori(0, H - 1) as h:
                head(h, h + 1)
            head(H - 1, None)
            act.wait_ge(ln_v, 1)
            fn(lnsq, cT, ACT.Square).then_inc(ln_a, 1)
            act.wait_ge(sin_out, 16 * H)
            def take_queries(a):
                for d in two:
                    act.wait_ge(tiles_done, FIRST["att"] + max(6 * a - 2, 0) + d + 1)
                    fn(xqs[a % 2][:, d, :], ps[d][:, 0:TOKENS], ACT.Copy).then_inc(att_q, 1)

            take_queries(0)
            act.wait_ge(ln_v, 2)
            fn(rs[:], rs[:], ACT.Sqrt).then_inc(ln_a, 1)
            act.wait_ge(ln_v, 3)
            fn(lnsq, cT, ACT.Tanh).then_inc(ln_a, 1)
            for a in range(AH):
                act.wait_ge(mx_ready, a + 1)
                for t in range(UNITS):
                    n = P if t < 2 else NS
                    src = ps[2][:, t * MEM:(t + 1) * MEM] if t < 2 else ps[3][0:n, 0:MEM]
                    last = fn(pp[0:n, t, :], src, ACT.Exp, bias=mx[0:n, t:t + 1], scale=1.0 / 16.0, accum_out=sm[0:n, t:t + 1])
                last.then_inc(pexp_ready, 1)
                if a + 1 < AH:
                    take_queries(a + 1)
                act.wait_ge(pt_done, a + 1)
                fn(pT[:, :, 0:TP], ps[6].rearrange("p (m t) -> p m t", m=2), ACT.Copy).then_inc(pt_ready, 1)
            with act.Fori(0, KT) as i:
                for n in range(3):
                    act.wait_ge(tiles_done, FIRST["merge"] + 5 * i + 2 * n + 1)
                    act.wait_ge(merge_read[n], i)
                    fn(g3[:, n, :], ps[2 * n][:, 0:TOKENS], ACT.Tanh, scale=0.5).then_inc(gate_done, 1)
            with act.Fori(0, 4) as i:
                for j in range(4):
                    act.wait_ge(out_read[j % 2], 2 * i + j // 2 + 1)
                    fn(hT[:, 4 * i + j, :], xT[:, 4 * i + j, :], ACT.Square).then_inc(x2_squared, 1)
            rooted(3, TOKENS)
            for t in range(UNITS):
                n = P if t < 2 else NS
                for q in range(4):
                    act.wait_ge(turned, 4 * t + q + 1)
                    fn(x2tok[0:n, t, q * 512:(q + 1) * 512], ps[q][0:n, :], ACT.Copy).then_inc(turned_read, 1)
            act.wait_ge(turned_read, 12)
            for t in range(UNITS):
                n = P if t < 2 else NS
                last = fn(seven[0:n, :], x2tok[0:n, t, :], ACT.Square, accum_out=r3[0:n, t:t + 1])
                last.then_inc(r3_a, 1)
                act.wait_ge(r3_a, t + 1)
            act.wait_ge(r3_v, 1)
            fn(r3[:], r3[:], ACT.Sqrt).then_inc(r3_a, 1)

            def soften(n):
                act.wait_ge(soft_in, n + 1)
                fn(gx[:, :, :], gx[:, :, :], ACT.Exp).then_inc(soft_out, 1)

            def lookups(i, first=False):
                for j in range(4):
                    b, n = j % 2, 2 * i + j // 2
                    act.wait_ge(tiles_done, FIRST["pq"] + 4 * i + j + 1)
                    act.wait_ge(scores_done[b], n)
                    fn(qs[:, b, :], ps[4 + b][:, 0:TOKENS], ACT.Copy).then_inc(q_read[b], 1)
                    act.wait_ge(scores_done[b], n + 1)
                    act.wait_ge(topk_read[j // 2], i)
                    for t in range(UNITS):
                        w = P if t < 2 else NS
                        last = fn(sc[0:w, j, t * P:(t + 1) * P], ps[6 + b][0:w, t * P:(t + 1) * P], ACT.Copy)
                    last.then_inc(scores_read[b], 1)
                    if not first:
                        if j == 0:
                            soften(2 * i - 1)
                        if j < 3:
                            t = i - 1
                            act.wait_ge(rest_ready, 3 * t + j + 1)
                            act.wait_ge(parts_out, 16 * t)
                            fn(parts[:, j, :], h2, ACT.Copy).then_inc(part_taken, 1)
                        if j == 2:
                            act.wait_ge(part_taken, 3 * t + 3)
                            act.dma_start(hparts[bass.ds(P * t, P)], parts[:, :, :]).then_inc(parts_out, 16)
                    if j == 3:
                        soften(2 * i)

            lookups(0, first=True)
            with act.Fori(1, 4) as i:
                lookups(i)
            soften(PH - 1)
            def weigh(i, r):
                g_, j = r // group, r % group
                n = 16 * i + r
                act.wait_ge(dotted[1], n + 1 + SLOTS)
                fn(ge[:, g_, j:j + 1], dots[:, g_, j, 0:1], ACT.Gelu_apprx_tanh, bias=dots[:, g_, j, 1:2]).then_inc(ge_ready, 1)
                act.wait_ge(ge_ready, n + 1)
                fn(wz[:, g_, j, j:j + 1], ge[:, g_, j:j + 1], ACT.Copy, scale=g8[:, g_, j:j + 1]).then_inc(w_ready, 1)

            def store_group(i, g_):
                act.wait_ge(summed, 16 * i + group * (g_ + 1) + SLOTS)
                act.wait_ge(experts_out[g_], 16 * i)
                fn(osb[32 * g_:32 * g_ + group, :].rearrange("p (q n) -> p q n", q=4), psum[32 * g_:32 * g_ + group, 4:8, :], ACT.Copy)\
                    .then_inc(acc_read[g_], 1)
                act.wait_ge(acc_read[g_], i + 1)
                act.dma_start(experts[bass.ds(16 * i + 8 * g_, group)], osb[32 * g_:32 * g_ + group, :]).then_inc(experts_out[g_], 16)

            def act_pair(i, first=False):
                for g_ in two:
                    if not first or g_:
                        act.wait_ge(w_ready, 16 * i + 8 * g_)
                    fn(g8[:, g_, :], gT[:, bass.ds(16 * i + 8 * g_, group)] if not first else gT[:, 8 * g_:8 * g_ + 8], ACT.Copy)\
                        .then_inc(g8_ready, 1)
                    act.wait_ge(g8_ready, 2 * i + g_ + 1)
                    for j in range(group):
                        weigh(i, group * g_ + j)
                        if j == 1:
                            if g_:
                                store_group(i, 0)
                            elif not first:
                                store_group(i - 1, 1)

            act.wait_ge(lists_ready, 2)
            act_pair(0, first=True)
            for t, (start, end) in enumerate(SPANS):
                with act.Fori(max(start, 1), end) as i:
                    act_pair(i)
                if t == 2:
                    store_group(PAIRS - 1, 1)
                n = P if t < 2 else NS
                act.wait_ge(r3_v, 3 + 3 * t)
                fn(h2[0:n, :], fy[0:n, :], ACT.Square, accum_out=r3[0:n, t:t + 1]).then_inc(r3_a, 1)
                act.wait_ge(r3_v, 4 + 3 * t)
                fn(r3[0:n, t:t + 1], r3[0:n, t:t + 1], ACT.Sqrt).then_inc(r3_a, 1)
                act.wait_ge(r3_v, 5 + 3 * t)
                act.dma_start(io["y"][t * P:t * P + n], fy[0:n, :]).then_inc(in_late, 16)

        @block.vector
        def _(dve):
            v = nc.vector
            st = Steps(dve, dve_step)

            def finish_norm(n, src, dst, gains, cols, bank, width):
                dve.wait_ge(ss_done, n)
                v.tensor_scalar(rs[:, 0:cols], ps[bank][:, 0:cols], 1.0 / width, EPS, ALU.mult, ALU.add).then_inc(ms_ready, 1)
                dve.wait_ge(rt_ready, n)
                st(v.reciprocal(rs[:, 0:cols], rs[:, 0:cols]))
                st.wait()
                for kt in range(KT):
                    last = v.scalar_tensor_tensor(dst[:, kt, 0:cols], src[:, kt, 0:cols], cst[:, gains + kt:gains + kt + 1],
                                                  rs[:, 0:cols], ALU.mult, ALU.mult)
                last.then_inc(norm_ready, 1)

            st(v.memset(ab[:, :, :], 0.0))
            st(v.memset(cwin[:, :, 0:CK - 1], 0.0))
            dve.wait_ge(in_cst, 16)
            finish_norm(1, mm, mm, C_MEM, MEM, 6, D)
            dve.wait_ge(norm_ready, 1)
            finish_norm(2, xT, hT, C_MIX, TOKENS, 7, D)
            st(v.tensor_scalar(half[:, 0:CT], cst[:, C_LNB:C_LNB + CT], 0.5, None, ALU.mult))
            st(v.tensor_scalar(half[:, CT:CT + 1], cst[:, C_DNG:C_DNG + 1], 0.5, None, ALU.mult))
            for g in range(4):
                dve.wait_ge(v_turned, g + 1)
                for q in range(4):
                    c, m = 2 * g + q // 2, q % 2
                    last = v.tensor_copy(vmem[:, m, c * P:(c + 1) * P], ps[g % 2][:, q * P:(q + 1) * P])
                last.then_inc(v_placed, 1)
            with dve.Fori(0, 4) as i:
                st.enter(i, 2 * (2 * CK + 2))
                for q in range(2):
                    c = 2 * i + q
                    dve.wait_ge(gate_ready[q], i + 1)
                    st(v.tensor_scalar(sg[:, q, :], sg[:, q, :], 0.5, 0.5, ALU.mult, ALU.add))
                    dwp = dwp2[:, q, :]
                    dve.wait_ge(conv_read[q], i)
                    st(v.tensor_copy(dwp[:, 0:CK], cst[:, bass.ds(C_DW + c * CK, CK)]))
                    st(v.tensor_copy(dwp[:, CK:CK + 1], cst[:, bass.ds(C_DWB + c, 1)]))
                    st.wait()
                    prompt = cwin[:, q, 0:CK - 1 + TP]
                    sample = cwin[:, q, CK - 1 + TP:].rearrange("p (b s) -> p b s", b=NBATCH)
                    v.tensor_tensor(prompt[:, CK - 1:], ps[4 + 2 * q][:, 0:TP], sg[:, q, 0:TP], ALU.mult)
                    dve.wait_ge(cwin_in[q], 16 * i + 16)
                    v.tensor_tensor(sample[:, :, CK - 1:], ps[4 + 2 * q][:, TP:TOKENS].rearrange("p (b s) -> p b s", b=NBATCH),
                                    sg[:, q, TP:].rearrange("p (b s) -> p b s", b=NBATCH), ALU.mult).then_inc(cwin_full[q], 1)
                    dve.wait_ge(cwin_full[q], i + 1)
                    out_p = cT[:, c, 0:TP]
                    out_s = cT[:, c, TP:TOKENS].rearrange("p (b s) -> p b s", b=NBATCH)
                    acc_p, acc_s = sg[:, q, 0:TP], sg[:, q, TP:].rearrange("p (b s) -> p b s", b=NBATCH)
                    for t in range(CK):
                        w = dwp[:, t:t + 1]
                        last_tap = t == CK - 1
                        for src, acc_, out_ in ((prompt[:, t:t + TP], acc_p, out_p), (sample[:, :, t:t + TS], acc_s, out_s)):
                            if t == 0:
                                ins = v.tensor_scalar(acc_, src, w, dwp[:, CK:CK + 1], ALU.mult, ALU.add)
                            else:
                                st.wait(st.n - 1)
                                ins = v.scalar_tensor_tensor(out_ if last_tap else acc_, src, w, acc_, ALU.mult, ALU.add)
                            if last_tap and acc_ is acc_s:
                                ins.then_inc(conv_read[q], 1)
                            else:
                                st(ins)
                st.leave(4)
            def uh(x):
                return x.rearrange("p (u h) -> p u h", u=UNITS)

            def hu(at_, n=UNITS):
                return hp[:, :, at_:at_ + n].rearrange("p h u -> p u h")

            raw, beta = uh(sp3[:, 2, :]), uh(sp3[:, 3, :])
            dve.wait_ge(in_rows, 16)
            dve.wait_ge(sp_a, 1)
            dt_row = rows[:, 16:32].unsqueeze(1).to_broadcast([P, UNITS, 16])
            st(v.tensor_tensor(raw, ab[:, :, 0:16], dt_row, ALU.add))
            v.tensor_copy(beta, ab[:, :, 16:32])
            st.wait()
            st(v.tensor_scalar(sp3[:, 1, :], sp3[:, 2, :], -1.0, None, ALU.mult))
            st.wait()
            st(v.tensor_tensor(sp3[:, 0, :], sp3[:, 1, :], sp3[:, 2, :], ALU.max))
            v.tensor_scalar(sp3[:, 2, :], sp3[:, 2, :], 0.0, None, ALU.max).then_inc(sp_v, 1)
            dve.wait_ge(sp_s, 2)
            v.tensor_scalar(sp3[:, 1, :], sp3[:, 1, :], 1.0, None, ALU.add).then_inc(sp_v, 1)
            dve.wait_ge(sp_s, 4)
            st(v.tensor_tensor(sp3[:, 2, :], sp3[:, 2, :], sp3[:, 1, :], ALU.add))
            st(v.tensor_scalar(sp3[:, 3, :], sp3[:, 3, :], 0.5, 0.5, ALU.mult, ALU.add))
            st.wait()
            st(v.scalar_tensor_tensor(uh(gz[:, 0:48]), raw, -1.0, rows[:, 0:16].unsqueeze(1).to_broadcast([P, UNITS, 16]),
                                      ALU.mult, ALU.mult))
            st.wait()
            st(v.memset(gz[NS:P, 32:48], 0.0))
            st.wait()
            v.tensor_tensor(gz[:, 48:].rearrange("p (b h) -> p b h", b=NBATCH),
                            gz[:, 32:48].unsqueeze(1).to_broadcast([P, NBATCH, H]),
                            bm[:].unsqueeze(2).to_broadcast([P, NBATCH, H]), ALU.mult).then_inc(ab_ready, 1)
            dve.wait_ge(sp_b, 1)
            st(v.tensor_copy(ex[:, 0:48], ps[4][:, 0:48]))
            st.wait()
            v.tensor_copy(ex[:, 96:144], ps[4][:, 48:96])
            v.tensor_copy(ex[:, 144:], ps[4][:, 96:96 + P])
            v.tensor_tensor(ex[:, 48:96], ps[4][:, 48:96], ex[:, 0:48], ALU.subtract)
            v.tensor_copy(hu(GC), uh(ps[4][:, 0:48])).then_inc(sp_v, 1)
            v.tensor_copy(hu(BETA), beta)
            v.tensor_copy(hu(GRAW), uh(gz[:, 0:48]))
            for pad in (qn, kn, vv):
                v.memset(pad[:, TOKENS:], 0.0)
            v.memset(knm, 0.0)
            dve.wait_ge(sp_s, 5)
            v.scalar_tensor_tensor(hu(NBEG), uh(ex[:, 0:48]), -1.0, beta, ALU.mult, ALU.mult)
            v.tensor_copy(hu(KDEC), uh(ex[:, 48:96]))
            v.tensor_copy(hu(EGL, 2), uh(ex[:, 96:144])[:, 0:2, :])
            v.tensor_copy(hu(EGLB, NBATCH), ex[:, 144:].rearrange("p (b h) -> p b h", b=NBATCH)).then_inc(sp_c, 1)
            v.memset(qwin[:, :, 0:QK - 1], 0.0).then_inc(sp_c, 1)
            dve.wait_ge(sp_c, 2)

            def taps(h):
                st(v.tensor_scalar(pw[:], cst[:, bass.ds(C_DNW + h * 3 * QK, 3 * QK)], 0.5, None, ALU.mult))

            def convolve(h, j, ts):
                if ts[0] == 0:
                    dve.wait_ge(proj_read[j], h + 1)
                prompt = qwin[:, j, 0:QWIN0]
                sample = qwin[:, j, QWIN0:].rearrange("p (b s) -> p b s", b=NBATCH)
                acc_p, acc_s = cv[:, j, 0:TP], cv[:, j, TP:].rearrange("p (b s) -> p b s", b=NBATCH)
                for t in ts:
                    w = pw[:, j * QK + t:j * QK + t + 1]
                    for src, acc_ in ((prompt[:, t:t + TP], acc_p), (sample[:, :, t:t + TS], acc_s)):
                        if t == 0:
                            ins = v.tensor_scalar(acc_, src, w, None, ALU.mult)
                        else:
                            st.wait(st.n - 1)
                            ins = v.scalar_tensor_tensor(acc_, src, w, acc_, ALU.mult, ALU.add)
                        if t == QK - 1 and acc_ is acc_s:
                            ins.then_inc(conv_ready, 1)
                        else:
                            st(ins)

            def silu(h, j):
                dve.wait_ge(tanh_ready, 3 * h + j + 1)
                out_ = cv[:, j, :] if j < 2 else vv[:, 0:TOKENS]
                v.scalar_tensor_tensor(out_, th[:, j, :], 1.0, cv[:, j, :], ALU.add, ALU.mult)\
                    .then_inc(silu_ready if j < 2 else v_ready, 1)

            def guarded(h):
                dve.wait_ge(ssq_done, h + 1)
                for n in two:
                    last = v.tensor_scalar(nrm[:, n, :], ps[n][:, 0:TOKENS], EPS, None, ALU.add)
                last.then_inc(nrm_ready, 1)

            def inverted(h):
                dve.wait_ge(nrt_ready, h + 1)
                st(v.reciprocal(nrm[:, :, :], nrm[:, :, :]))

            def head(h, nxt):
                h1 = h + 1
                st(v.tensor_copy(hs[:], hp[:, h, :]))
                st.wait()
                if nxt is not None:
                    taps(nxt)
                st(v.tensor_tensor(kn[:, 0:TOKENS], cv[:, 1, :], nrm[:, 1, :], ALU.mult))
                v.scalar_tensor_tensor(qn[:, 0:TOKENS], cv[:, 0, :], float(P) ** -0.5, nrm[:, 0, :], ALU.mult, ALU.mult)\
                    .then_inc(qk_ready, 1)
                st.wait()
                v.tensor_copy(knm.rearrange("p (b s) -> p b s", s=72)[:, :, 0:TS],
                              kn[:, TP:TOKENS].rearrange("p (b s) -> p b s", b=NBATCH)).then_inc(knm_ready, 1)
                dve.wait_ge(rows_done, h1)
                for u in range(UNITS):
                    last = v.tensor_scalar(dt3[:, u, :], ps[7][:, u * P:(u + 1) * P], hs[:, GC + u:GC + u + 1], 0.0,
                                           ALU.subtract, ALU.min)
                last.then_inc(dt_ready, 1)
                dve.wait_ge(z_ready, h1)
                v.scalar_tensor_tensor(zs, zs, 1.0, ps[3][:, 0:TOKENS], ALU.add, ALU.mult).then_inc(proj_read[3], 1)
                dve.wait_ge(dtx_ready, h1)
                st(v.tensor_tensor(dt3[:, :, :], dt3[:, :, :], mu3[:, :, :], ALU.mult))
                st.wait()
                v.tensor_tensor(db3[:, :, :], dt3[:, :, :], three(6), ALU.mult).then_inc(rows_used, 1)
                dve.wait_ge(rows_used, 2 * h1)
                dve.wait_ge(g_done, h1)
                v.tensor_tensor(at3[:, :, :], three(4), db3[:, :, :], ALU.mult).then_inc(at_ready, 1)
                st(v.tensor_tensor(qkd[:, :, :], three(5), dt3[:, :, :], ALU.mult))
                v.tensor_tensor(qn, qn, egb[:], ALU.mult).then_inc(qd_ready, 1)
                dve.wait_ge(lt_ready, len(LEVELS) * h + 1)
                v.tensor_tensor(tt[:, :, :], ident[:].unsqueeze(1).to_broadcast([P, UNITS, P]),
                                lt[:, 0, :].rearrange("p (u n) -> p u n", u=UNITS), ALU.subtract).then_inc(t_ready, 1)
                dve.wait_ge(turn_done, h1)
                v.tensor_copy(tn[:, :, :], three(4)).then_inc(t_ready, 1)
                dve.wait_ge(tok_read, 2 * h1)
                dve.wait_ge(ks_done, 2 * h + 1)
                v.scalar_tensor_tensor(vb[0:NS, 2, :], ps[7][0:NS, 384:512], hs[0:NS, NBEG + 2:NBEG + 3], vb[0:NS, 2, :],
                                       ALU.mult, ALU.add).then_inc(r_ready, 1)
                for l in range(1, len(LEVELS)):
                    units = UNITS if l < SAMPLE_LEVELS else 2
                    if l < len(LEVELS) - 1:
                        dve.wait_ge(dd_done, 11 * h + 2 * l - 1)
                        v.tensor_tensor(tn[:, 0:units, :], tn[:, 0:units, :], three(5)[:, 0:units, :], ALU.subtract)\
                            .then_inc(t_ready, 1)
                    dve.wait_ge(dd_done, 11 * h + min(2 * l, 11))
                    v.tensor_tensor(tt[:, 0:units, :], tt[:, 0:units, :], three(6)[:, 0:units, :], ALU.subtract).then_inc(t_ready, 1)
                    if nxt is not None:
                        if l == 1:
                            dve.wait_ge(qk_ready, h1)
                            convolve(nxt, 0, range(2))
                        if l == 2:
                            convolve(nxt, 0, range(2, QK))
                        if l == 3:
                            convolve(nxt, 1, range(2))
                        if l == 4:
                            convolve(nxt, 1, range(2, QK))
                            silu(nxt, 0)
                        if l == 5:
                            silu(nxt, 1)
                if nxt is not None:
                    convolve(nxt, 2, range(QK))
                dve.wait_ge(ks_done, 2 * h + 2)
                v.scalar_tensor_tensor(vb[:, 1, :], ps[7][:, 2 * P:3 * P], hs[:, NBEG + 1:NBEG + 2], vb[:, 1, :],
                                       ALU.mult, ALU.add).then_inc(r_ready, 1)
                if nxt is not None:
                    guarded(nxt)
                    silu(nxt, 2)
                dve.wait_ge(so_done, h1)
                dve.wait_ge(s2_out, 16 * h)
                v.scalar_tensor_tensor(s2, s1, hs[:, EGL + 1:EGL + 2], ps[4][:, P:2 * P], ALU.mult, ALU.add)\
                    .then_inc(state_ready, 1)
                dve.wait_ge(sc_done, h1)
                dve.wait_ge(sn_done, 2 * h1)
                st(v.tensor_tensor(sin[:, 0:4, :], sin[:, 0:4, :], ps[6][:, :].rearrange("p (b e) -> p b e", b=4), ALU.add))
                v.tensor_tensor(sin[:, 4:8, :], sin[:, 4:8, :], ps[7][:, :].rearrange("p (b e) -> p b e", b=4), ALU.add)\
                    .then_inc(sn_ready, 1)
                if nxt is not None:
                    inverted(nxt)
                dve.wait_ge(oss_done, h1)
                v.tensor_scalar(rs[:], ps[4][:, 0:TOKENS], 1.0 / P, EPS, ALU.mult, ALU.add).then_inc(orm_ready, 1)
                dve.wait_ge(ort_ready, h1)
                st(v.reciprocal(rs[:], rs[:]))
                st.wait()
                st(v.tensor_tensor(rs[:], rs[:], ps[5][:, 0:TOKENS], ALU.mult))
                st.wait()
                v.scalar_tensor_tensor(oT[:, h, :], rs[:], half[:, CT:CT + 1], zs, ALU.mult, ALU.mult).then_inc(o_done, 1)

            taps(0)
            st.wait()
            for j in range(3):
                convolve(0, j, range(QK))
            for j in range(3):
                silu(0, j)
            guarded(0)
            inverted(0)
            st.wait()
            with dve.Fori(0, H - 1) as h:
                st.enter(h, HEAD_STEPS)
                head(h, h + 1)
                st.leave(H - 1)
            head(H - 1, None)
            dve.wait_ge(ln_done, 1)
            st(v.tensor_scalar(mean[:], ps[4][:, 0:TOKENS], 1.0 / 1024, None, ALU.mult))
            st.wait()
            over = mean[:].unsqueeze(1).to_broadcast([P, CT, TOKENS])
            v.tensor_tensor(cT, cT, over, ALU.subtract).then_inc(ln_v, 1)
            st(v.memset(r3[:], 1.0))
            st(v.memset(seven[:, 0:2 * 576], 0.0))
            st.wait()
            def sample_queries(a):
                dve.wait_ge(att_q, 2 * a + 2)
                for d in two:
                    last = v.tensor_copy(qm[:, d, :].rearrange("p (b s) -> p b s", s=72)[:, :, 0:TS],
                                         xqs[a % 2][:, d, TP:].rearrange("p (b s) -> p b s", b=NBATCH))
                last.then_inc(qm_ready, 1)

            sample_queries(0)
            dve.wait_ge(ln_done, 2)
            v.tensor_scalar(rs[:], ps[5][:, 0:TOKENS], 1.0 / 1024, EPS, ALU.mult, ALU.add).then_inc(ln_v, 1)
            dve.wait_ge(ln_a, 2)
            st(v.reciprocal(rs[:], rs[:]))
            st.wait()
            st(v.scalar_tensor_tensor(cT, cT, 0.5, rs[:].unsqueeze(1).to_broadcast([P, CT, TOKENS]), ALU.mult, ALU.mult))
            st.wait()
            for c in range(CT):
                last = v.tensor_scalar(cT[:, c, :], cT[:, c, :], cst[:, C_LNG + c:C_LNG + c + 1], half[:, c:c + 1], ALU.mult, ALU.add)
            last.then_inc(ln_v, 1)
            dve.wait_ge(ln_a, 3)
            v.scalar_tensor_tensor(cT, lnsq, 1.0, cT, ALU.add, ALU.mult).then_inc(ln_v, 1)
            for a in range(AH):
                done = FIRST["att"] + 6 * a
                dve.wait_ge(tiles_done, done + 4)
                st(v.tensor_reduce(mx[:, 0:2], ps[2].rearrange("p (t m) -> p t m", t=2), AX, ALU.max))
                st(v.tensor_reduce(mx[0:NS, 2:3], ps[3][0:NS, 0:MEM], AX, ALU.max))
                st.wait()
                v.tensor_scalar(mx[:, 0:2], mx[:, 0:2], -1.0 / 16.0, None, ALU.mult)
                v.tensor_scalar(mx[0:NS, 2:3], mx[0:NS, 2:3], -1.0 / 16.0, None, ALU.mult).then_inc(mx_ready, 1)
                dve.wait_ge(pexp_ready, a + 1)
                st(v.reciprocal(sm[:, 0:2], sm[:, 0:2]))
                st(v.reciprocal(sm[0:NS, 2:3], sm[0:NS, 2:3]))
                st.wait()
                for t in range(UNITS):
                    n = P if t < 2 else NS
                    last = v.tensor_scalar(pp[0:n, t, :], pp[0:n, t, :], sm[0:n, t:t + 1], None, ALU.mult)
                last.then_inc(pn_ready, 1)
                dve.wait_ge(pt_done, a + 1)
                v.tensor_copy(pT[:, :, TP:], ps[7][:, 0:P].rearrange("p (m t) -> p m t", m=2)).then_inc(pt_ready, 1)
                if a + 1 < AH:
                    sample_queries(a + 1)
                dve.wait_ge(tiles_done, min(done + 8, FIRST["att"] + 6 * AH))
                v.tensor_copy(xoT[:, 2 * a, :], ps[4][:, 0:TOKENS])
                v.tensor_copy(xoT[:, 2 * a + 1, :], ps[5][:, 0:TOKENS]).then_inc(ao_read, 1)
            dve.wait_ge(s2_out, 16 * H)
            with dve.Fori(0, KT) as i:
                st.enter(i, 1)
                dve.wait_ge(merged_ready, i)
                for n, (bank, tile) in enumerate(((1, 2), (3, 4), (5, 5))):
                    dve.wait_ge(gate_done, 3 * i + n + 1)
                    dve.wait_ge(tiles_done, FIRST["merge"] + 5 * i + tile)
                    v.scalar_tensor_tensor(t3[:, n, :], g3[:, n, :], 1.0, ps[bank][:, 0:TOKENS], ALU.add, ALU.mult).then_inc(merge_read[n], 1)
                    if n == 1:
                        dve.wait_ge(merge_read[1], i + 1)
                        st(v.tensor_tensor(t3[:, 0, :], t3[:, 0, :], t3[:, 1, :], ALU.add))
                dve.wait_ge(merge_read[2], i + 1)
                st.wait()
                v.tensor_tensor(mm[:, i, :], t3[:, 0, :], t3[:, 2, :], ALU.add).then_inc(merged_ready, 1)
                st.leave(KT)
            with dve.Fori(0, 4) as i:
                for j in range(4):
                    dve.wait_ge(tiles_done, FIRST["out"] + 4 * i + j + 1)
                    x = xT[:, 4 * i + j, :]
                    v.scalar_tensor_tensor(x, ps[6 + j % 2][:, 0:TOKENS], 0.5, x, ALU.mult, ALU.add).then_inc(out_read[j % 2], 1)
            finish_norm(3, xT, hT, C_FFN, TOKENS, 5, D)
            dve.wait_ge(r3_a, 3)
            dve.wait_ge(norm_ready, 3)
            dve.wait_ge(consts_ready, 2)
            st(v.memset(sc[NS:P, :, 2 * P:], 0.0))
            v.memset(wz[:, :, :, :], 0.0).then_inc(dotted[0], SLOTS)
            v.memset(efull[:, :, :], 0.0).then_inc(dotted[1], SLOTS)
            v.tensor_scalar(r3[:], r3[:], 1.0 / D, EPS, ALU.mult, ALU.add).then_inc(r3_v, 1)
            dve.wait_ge(r3_a, 4)
            v.reciprocal(r3[:], r3[:]).then_inc(r3_v, 1)
            st.wait()
            combos = [(x, t) for x in two for t in range(UNITS)]
            with dve.Fori(0, 4) as i:
                st.enter(i, TOPK_STEPS)
                for q in two:
                    head_at = (2 * i + q) * TOPK
                    dve.to_reg(2 * i + q + 1)
                    dve.wait_ge(r3_a, 4)
                    for x in two:
                        dve.wait_ge(scores_read[x], 2 * i + q + 1)

                    def lst(x, t):
                        return sc[:, 2 * q + x, t * P:(t + 1) * P]

                    def lst2(x, t):
                        return sc2[:, x, t * P:(t + 1) * P]

                    for x, t in combos:
                        st(v.max(v16[:, x, t, 0:8], lst(x, t)))
                    st.wait_after(r3_a, 4)
                    for x, t in combos:
                        st(v.max_index(iu[:, x, t, 0:8], v16[:, x, t, 0:8], lst(x, t)))
                    for x, t in combos:
                        st(v.match_replace(lst2(x, t), v16[:, x, t, 0:8], lst(x, t), NEG))
                    st.wait_after(r3_a, 4)
                    for x, t in combos:
                        st(v.max(v16[:, x, t, 8:16], lst2(x, t)))
                    st.wait_after(r3_a, 4)
                    for n, (x, t) in enumerate(combos):
                        st(v.max_index(iu[:, x, t, 8:16], v16[:, x, t, 8:16], lst2(x, t)))
                    st(v.tensor_tensor(cand[:, :, :].rearrange("p t (a b) -> p t a b", a=TOPK),
                                       v16[:, 0].unsqueeze(3).to_broadcast([P, UNITS, TOPK, TOPK]),
                                       v16[:, 1].unsqueeze(2).to_broadcast([P, UNITS, TOPK, TOPK]), ALU.add))
                    st.wait()
                    v.tensor_copy(i16, iu).then_inc(topk_read[q], 1)
                    for t in range(UNITS):
                        st(v.max(top[:, t, 0:8], cand[:, t, :]))
                    st.wait_after(r3_a, 4)
                    for t in range(UNITS):
                        st(v.max_index(pos[:, t, 0:8], top[:, t, 0:8], cand[:, t, :]))
                        st(v.match_replace(cand2[:, t, :], top[:, t, 0:8], cand[:, t, :], NEG))
                    st.wait_after(r3_a, 4)
                    for t in range(UNITS):
                        st(v.max(top[:, t, 8:16], cand2[:, t, :]))
                    st.wait_after(r3_a, 4)
                    for t in range(UNITS):
                        st(v.max_index(pos[:, t, 8:16], top[:, t, 8:16], cand2[:, t, :]))
                    v.tensor_tensor(gx[:, :, :], top[:, :, :], top[:, :, 0:1].to_broadcast([P, UNITS, TOPK]), ALU.subtract)\
                        .then_inc(soft_in, 1)
                    st.wait()
                    flat = pos[:, :, :].rearrange("p t k -> p (t k)")
                    st(v.tensor_scalar(digits[:, 0, :], flat, 4, None, ALU.logical_shift_right))
                    st(v.tensor_scalar(digits[:, 1, :], flat, 15, None, ALU.bitwise_and))
                    st.wait()
                    st(v.tensor_copy(fdig[:, :, :], digits[:, :, :]))
                    st.wait()
                    for x in two:
                        st(v.tensor_tensor(eq, fdig[:, x, :].unsqueeze(2).to_broadcast([P, UNITS * TOPK, TOPK]),
                                           iota16[:].unsqueeze(1).to_broadcast([P, UNITS * TOPK, TOPK]), ALU.is_equal))
                        st.wait()
                        e4 = eq.rearrange("p (t k) r -> p t k r", t=UNITS)
                        st(v.tensor_tensor(e4, e4, i16[:, x].unsqueeze(2).to_broadcast([P, UNITS, TOPK, TOPK]), ALU.mult))
                        st.wait()
                        st(v.tensor_reduce(e12[:, x, :], eq, AX, ALU.add))
                        st.wait()
                    st(v.scalar_tensor_tensor(efull[:, :, bass.ds(head_at, TOPK)], e12[:, 0, :].rearrange("p (t k) -> p t k", t=UNITS),
                                              float(NK), e12[:, 1, :].rearrange("p (t k) -> p t k", t=UNITS), ALU.mult, ALU.add))
                    dve.wait_ge(soft_out, 2 * i + q + 1)
                    st(v.tensor_reduce(gsum, gx[:, :, :], AX, ALU.add))
                    st.wait()
                    st(v.reciprocal(gsum, gsum))
                    st.wait()
                    v.tensor_tensor(gfull[:, :, bass.ds(head_at, TOPK)], gx[:, :, :],
                                    gsum.unsqueeze(2).to_broadcast([P, UNITS, TOPK]), ALU.mult).then_inc(picked, 1)
                    dve.wait_ge(picked, 2 * i + q + 1)
                st.leave(4)
            dve.wait_ge(lists_turned, 1)
            v.tensor_copy(eT, ps[0][:, 0:TOKENS]).then_inc(lists_ready, 1)
            v.tensor_copy(gT, ps[1][:, 0:TOKENS]).then_inc(lists_ready, 1)
            for t, (start, end) in enumerate(SPANS):
                with dve.Fori(start, end) as i:
                    for r in range(2 * group):
                        s, g_, j = r % 4, r // group, r % group
                        dve.wait_ge(u_in[s], 64 * i + 16 * (r // 4) + 16)
                        for half_ in two:
                            dve.wait_ge(spread, 32 * i + 2 * r + half_ + 1 + 2 * SLOTS)
                            u = ring[:, s, half_ * 1024:(half_ + 1) * 1024]
                            x = psum[:, 2 * half_:2 * half_ + 2, :].rearrange("p b n -> p (b n)")
                            v.tensor_tensor_reduce(out=u, in0=u, in1=x, scale=1.0, scalar=0.0, op0=ALU.mult, op1=ALU.add,
                                                         accum_out=dots[:, g_, j, half_:half_ + 1]).then_inc(dotted[half_], 1)
                n = P if t < 2 else NS
                y = fy[0:n, :]
                dve.wait_ge(parts_out, 64 + 16 * t)
                v.tensor_tensor(y, y, x2tok[0:n, t, :], ALU.add).then_inc(r3_v, 1)
                dve.wait_ge(r3_a, 4 + 2 * t + 1)
                v.tensor_scalar(r3[0:n, t:t + 1], r3[0:n, t:t + 1], 1.0 / D, EPS, ALU.mult, ALU.add).then_inc(r3_v, 1)
                dve.wait_ge(r3_a, 4 + 2 * t + 2)
                st(v.reciprocal(r3[0:n, t:t + 1], r3[0:n, t:t + 1]))
                st.wait()
                dve.wait_ge(in_late, 48)
                v.scalar_tensor_tensor(y, y, r3[0:n, t:t + 1], grow[0:n, :], ALU.mult, ALU.mult).then_inc(r3_v, 1)

        @block.gpsimd
        def _(pool):
            g = nc.gpsimd
            st = Steps(pool, pool_step)

            def select(out, pattern, base, mult, op=ALU.is_ge, fill=0.0):
                st.wait()
                st(g.affine_select(out=out, in_=out, compare_op=op, fill=fill, base=base, pattern=pattern, channel_multiplier=mult))

            st(g.memset(ones[:], 1.0))
            st.wait()
            g.memset(sin, 0.0).then_inc(consts_ready, 1)
            st(g.memset(ident[:], 0.0))
            select(ident[:], [[-1, P]], 0, 1, ALU.not_equal, 1.0)
            st(g.memset(mu3[:, :, :], 1.0))
            st(g.memset(blk[:], 1.0))
            st(g.memset(bm[:], 1.0))
            st(g.memset(lm[:, :, :], 0.0))
            select(mu3[:, :, :], [[0, UNITS], [1, P]], 0, -1)
            nb = P // TS
            for m in (blk[:], mu3[:, 2, :]):
                grid = m.rearrange("p (n s) -> p n s", s=TS)
                select(grid, [[-TS, nb], [0, TS]], 0, 1)
                select(grid, [[TS, nb], [0, TS]], TS - 1, -1)
            select(bm[:], [[-TS, NBATCH]], 0, 1)
            select(bm[:], [[TS, NBATCH]], TS - 1, -1)
            for l, s in enumerate(LEVELS):
                low = lm[:, l, :].rearrange("p (n two s) -> p n two s", two=2, s=s)[:, :, 1, :]
                n = P // (2 * s)
                st.wait()
                st(g.memset(low, 1.0))
                select(low, [[-2 * s, n], [0, s]], 0, 1)
                select(low, [[2 * s, n], [0, s]], s - 1, -1)
            st(g.iota(iota16[:], [[1, TOPK]], base=0, channel_multiplier=0, allow_small_or_imprecise_dtypes=True))
            st(g.memset(onesb[:], 1.0))
            st.wait()
            g.memset(um, 0.0).then_inc(consts_ready, 1)
            pool.wait_ge(sp_c, 2)
            with pool.Fori(0, H) as h:
                h1 = h + 1
                st.enter(h, 1)
                pool.wait_ge(sc_done, h)
                pool.wait_ge(sp_c, 2)
                st(g.tensor_copy(hs_pool[:], hp[:, h, :]))
                st.wait()
                pool.wait_ge(rows_done, h)
                for out_, at_ in ((gb, GRAW), (bb, BETA)):
                    last = g.tensor_tensor(out_[:, :, :], ones[:].unsqueeze(1).to_broadcast([P, UNITS, P]),
                                           hs_pool[:, at_:at_ + UNITS].unsqueeze(2).to_broadcast([P, UNITS, P]), ALU.mult)
                last.then_inc(gb_ready, 1)
                pool.wait_ge(at_ready, h1)
                for l in range(len(LEVELS)):
                    units = UNITS if l < SAMPLE_LEVELS else 2
                    g.tensor_tensor(lt[:, l, 0:units * P].rearrange("p (u n) -> p u n", u=units), at3[:, 0:units, :],
                                    lm[:, l, :].unsqueeze(1).to_broadcast([P, units, P]), ALU.mult).then_inc(lt_ready, 1)
                pool.wait_ge(u_ready, 2 * h + 1)
                g.tensor_tensor(um, uu[:, 1, :].unsqueeze(1).to_broadcast([P, NBATCH, P]),
                                bm[:].unsqueeze(2).to_broadcast([P, NBATCH, P]), ALU.mult).then_inc(um_ready, 1)
                pool.wait_ge(so_done, h1)
                g.tensor_tensor(sin, sin, hs_pool[:, EGLB:EGLB + NBATCH].unsqueeze(2).to_broadcast([P, NBATCH, P]),
                                ALU.mult).then_inc(sc_done, 1)
                st.leave(H)
            pool.wait_ge(r3_v, 2)
            pool.wait_ge(in_late, 32)
            st(g.memset(x2tok[NS:P, 2, :], 0.0))
            st.wait()
            for t in range(UNITS):
                if t:
                    pool.wait_ge(part_taken, 3 * t)
                st(g.tensor_scalar(h2, x2tok[:, t, :], r3[:, t:t + 1], None, ALU.mult))
                st.wait()
                g.tensor_tensor(h2, h2, grow, ALU.mult).then_inc(rest_ready, 1)
                for m in range(2):
                    pool.wait_ge(part_taken, 3 * t + m + 1)
                    pool.wait_ge(rest_ready, 3 * t + m + 1)
                    g.tensor_tensor(h2, h2, parts[:, m, :], ALU.subtract).then_inc(rest_ready, 1)
            pool.wait_ge(lists_ready, 2)
            with pool.Fori(0, PAIRS) as i:
                for g_ in two:
                    g.tensor_copy(idx8[:, g_, :], eT[:, bass.ds(16 * i + 8 * g_, group)]).then_inc(idx_ready, 1)
                    pool.wait_ge(idx_ready, 2 * i + g_ + 1)
                    for j in range(group):
                        s, n = j % 4, 16 * i + group * g_ + j
                        at_ = bass.IndirectOffsetOnAxis(ap=idx8[:, g_, j:j + 1], axis=0)
                        pool.to_reg(n + 1)
                        pool.wait_ge(lists_ready, 2)
                        pool.wait_ge(dotted[1], n + 1)
                        g.indirect_dma_start(ring[:, s, :], None, io["peer_u"], at_).then_inc(u_in[s], 16)
                        pool.wait_ge(lists_ready, 2)
                        pool.wait_ge(summed, n + 1)
                        g.indirect_dma_start(ring[:, 4 + s, :], None, io["peer_v"], at_).then_inc(v_in[s], 16)



def tiles(w):
    k, n = w.shape
    return np.ascontiguousarray(w.reshape(k // P, P, n // P, P).transpose(2, 1, 0, 3).reshape(n // P, P, k))


def cols(v):
    return v.reshape(-1, P).T


_OUTS = {"y": (TOKENS, D), "mem_k": (P, CT, MEM), "mem_v": (P, 2, 1024), "conv_out": (CT, P, CWIN), "qkv_out": (H, P, 3, QWIN),
         "delta_p": (H, P, P), "delta_s": (NBATCH, H, P, P)}


def layouts(a):
    w_in = a["w_in"][0]
    pieces = np.split(w_in, np.cumsum([1024, 1024, 6144, 2048, 16, 16, 1024, D, D]), axis=1)
    glu_a, glu_g, qkv, z, w_a, w_b, xq, g_conv, g_dn, g_xa = pieces
    x = np.concatenate([a["x_prompt"][0], a["x_sample"].reshape(NS, D)], 0)
    arr = {}
    arr["xT"] = x.T.reshape(KT, P, TOKENS).transpose(1, 0, 2)
    arr["memT"] = a["mem_prompt"][0].T.reshape(KT, P, MEM).transpose(1, 0, 2)
    dw = a["conv_dw"][0].T.reshape(CT, P, CK).transpose(1, 0, 2).reshape(P, CT * CK)
    dnw = a["dn_conv_w"][0].T.reshape(3, H, P, QK).transpose(2, 1, 0, 3).reshape(P, H * 3 * QK)
    arr["consts"] = np.concatenate([cols(a["norm_mem"][0]), cols(a["norm_mix"][0]), cols(a["norm_ffn"][0]), cols(a["conv_ln_g"][0]),
                                    cols(a["conv_ln_b"][0]), cols(a["conv_dw_b"][0]), dw, dnw, cols(a["dn_norm_g"][0])], 1)
    arr["dn_rows"] = np.concatenate([a["dn_a_log"][0], a["dn_dt_bias"][0]])
    arr["w_ab"] = np.concatenate([w_a, w_b], 1).reshape(KT, P, 32).transpose(1, 0, 2).reshape(P, KT * 32)
    arr["w_mem"] = tiles(a["w_mem_kv"][0])
    arr["w_glu"] = np.stack([tiles(glu_a), tiles(glu_g)], 1).reshape(2 * CT, P, D)
    q, k, v = (tiles(t) for t in np.split(qkv, 3, axis=1))
    arr["w_head"] = np.stack([q, k, v, tiles(z)], 1).reshape(4 * H, P, D)

    def windows(state, n_new):
        b, k1, c = state.shape
        s = state.transpose(2, 0, 1).reshape(c // P, P, b, k1)
        return np.concatenate([s, np.zeros(s.shape[:3] + (n_new,), s.dtype)], 3)

    arr["conv_in"] = windows(a["state_conv"][0], TS).reshape(CT, P, NBATCH * CWIN_S)
    arr["qkv_in"] = windows(a["state_qkv_conv"][0], TS).reshape(3, H, P, NBATCH * QWIN_S).transpose(1, 2, 0, 3)
    arr["delta_in"] = a["state_delta"][0]
    kc = a["cache_mem_k"][0].reshape(2, 4, MEM, AH, 2, P).transpose(3, 0, 5, 1, 4, 2).reshape(AH, 2, P, D)
    vc = a["cache_mem_v"][0].reshape(2, 4, 2, P, AH, 256).transpose(4, 0, 3, 1, 2, 5).reshape(AH, 2, P, D)
    xt = tiles(xq).reshape(AH, 2, P, D)
    order = [xt[0]]
    for h in range(AH):
        order += [kc[h]] + ([xt[h + 1]] if h + 1 < AH else []) + [vc[h]]
    arr["w_att"] = np.concatenate(order, 0)
    gates = [tiles(w) for w in (g_conv, g_dn, g_xa)]
    outer = np.concatenate([tiles(a["w_conv_out"][0]), tiles(a["w_xa_out"][0])], 2)
    arr["w_merge"] = np.stack([gates[0], outer, gates[1], tiles(a["w_dn_out"][0]), gates[2]], 1).reshape(5 * KT, P, D)
    arr["w_outp"] = tiles(a["w_out"][0])
    arr["w_pq"] = tiles(a["w_peer_q"][0])
    arr["keysT"] = np.stack([a["peer_keys_1"][0].T, a["peer_keys_2"][0].T], 1)
    arr["g_rows"] = np.stack([a["norm_ffn"][0], a["norm_final"]])
    arr["peer_u"] = a["peer_u"][0]
    arr["peer_v"] = a["peer_v"][0]
    return {k: np.ascontiguousarray(v) for k, v in arr.items()}


def results(o):
    y = o["y"]
    k = o["mem_k"].transpose(2, 1, 0).reshape(1, 1, MEM, AH, 256)
    v = o["mem_v"].transpose(1, 0, 2).reshape(1, 1, MEM, AH, 256)
    cw = o["conv_out"].reshape(1024, CWIN)
    conv_p = cw[:, TP:TP + CK - 1].T[None, None]
    conv_s = cw[:, CK - 1 + TP:].reshape(1024, NBATCH, CWIN_S)[:, :, TS:].transpose(1, 2, 0)[None]
    qw = o["qkv_out"].transpose(2, 0, 1, 3).reshape(3 * H * P, QWIN)
    qkv_p = qw[:, TP:TP + QK - 1].T[None, None]
    qkv_s = qw[:, QWIN0:].reshape(3 * H * P, NBATCH, QWIN_S)[:, :, TS:].transpose(1, 2, 0)[None]
    out = (y[:TP].reshape(1, TP, D), y[TP:].reshape(NBATCH, TS, D), k, v, conv_p, qkv_p,
           o["delta_p"].reshape(1, 1, H, P, P), conv_s, qkv_s, o["delta_s"].reshape(1, NBATCH, H, P, P))
    return tuple(np.ascontiguousarray(x) for x in out)


def kernel(**inputs):
    import concourse.bacc as bacc
    from concourse.bass_utils import run_bass_kernel_spmd

    nc = bacc.Bacc("TRN2", target_bir_lowering=False, num_devices=1)
    arrays = layouts({k: np.asarray(v) for k, v in inputs.items()})
    io = {k: nc.dram_tensor(f"in_{k}", v.shape, F32, kind="ExternalInput").ap() for k, v in arrays.items()}
    for k, shape in _OUTS.items():
        io[k] = nc.dram_tensor(f"out_{k}", shape, F32, kind="ExternalOutput").ap()
    build(nc, io)
    r = run_bass_kernel_spmd(nc, [{f"in_{k}": v for k, v in arrays.items()}], core_ids=[0])
    return results({k: r.results[0][f"out_{k}"] for k in _OUTS})
```
